# Optimizing a Trainium2 kernel written in Bass

```python
import math
import jax, jax.numpy as jnp
from jax import lax
import numpy as np

D_MODEL = 2048
BATCH = 1
SEQ = 256
DEPTH = 1
DEC_BATCH = 8
DEC_SEQ = 8
PAST_LEN = 1024
PAGE_SIZE = 128

N_META = 16
N_HEADS = 8
HEAD_DIM = 128
ATTN_WIDTH = N_HEADS * HEAD_DIM
IDX_HEADS = 16
IDX_DIM = 64
TOPK_MAX = 256
Q_BLOCK = 128
REL_BUCKETS = 32
REL_MAX_DIST = 128
CONV_CH = 1024
CONV_WIDTH = 31
CONV_CTX = CONV_WIDTH - 1
FF_RAW = -(-8 * D_MODEL // 3)
D_FF = -(-FF_RAW // 256) * 256
D_IN = 3 * ATTN_WIDTH + IDX_HEADS * IDX_DIM + IDX_DIM + IDX_HEADS + 2 * CONV_CH + 2 * D_MODEL
NORM_EPS = 1e-6
MASK_VALUE = -1e30

kernel_name = 'hybrid_dsa_conformer_decode_step'

def rmsnorm(x, g):
    xf = x.astype(jnp.float32)
    y = xf * lax.rsqrt(jnp.mean(xf * xf, axis=-1, keepdims=True) + NORM_EPS)
    return (y * g.astype(jnp.float32)).astype(x.dtype)

def layernorm(x, g, b):
    xf = x.astype(jnp.float32)
    mu = jnp.mean(xf, axis=-1, keepdims=True)
    var = jnp.mean(jnp.square(xf - mu), axis=-1, keepdims=True)
    y = (xf - mu) * lax.rsqrt(var + NORM_EPS)
    return (y * g.astype(jnp.float32) + b.astype(jnp.float32)).astype(x.dtype)

def t5_bucket(rel):
    n = jnp.maximum(rel, 0)
    max_exact = REL_BUCKETS // 2
    nf = jnp.maximum(n, 1).astype(jnp.float32)
    large = max_exact + (jnp.log(nf / max_exact) / math.log(REL_MAX_DIST / max_exact)
                         * (REL_BUCKETS - max_exact)).astype(jnp.int32)
    large = jnp.minimum(large, REL_BUCKETS - 1)
    return jnp.where(n < max_exact, n, large)

def take_rows(a, idx):
    return jax.vmap(lambda ab, ib: ab[ib])(a, idx)

def index_scores(iq, iw, ik, q_pos, k_pos):
    s = jnp.einsum('bqhd,bkd->bqhk', iq, ik).astype(jnp.float32) * (IDX_DIM ** -0.5)
    s = jnp.einsum('bqhk,bqh->bqk', jax.nn.relu(s), iw.astype(jnp.float32)) * (IDX_HEADS ** -0.5)
    return jnp.where(k_pos[None, None, :] <= q_pos[None, :, None], s, -jnp.inf)

def sparse_attend(q, k_sel, v_sel, q_pos, k_pos_sel, rel_bias):
    logits = jnp.einsum('bqhd,bqkhd->bhqk', q, k_sel).astype(jnp.float32) * (HEAD_DIM ** -0.5)
    rel = q_pos[None, :, None] - k_pos_sel
    bias = jnp.moveaxis(rel_bias.astype(jnp.float32)[t5_bucket(rel)], -1, 1)
    logits = jnp.where((rel >= 0)[:, None], logits + bias, MASK_VALUE)
    p = jax.nn.softmax(logits, axis=-1).astype(v_sel.dtype)
    return jnp.einsum('bhqk,bqkhd->bqhd', p, v_sel)

def mixer_inputs(x, g_norm, w_in, q_g, k_g):
    B, T = x.shape[0], x.shape[1]
    xn = rmsnorm(x, g_norm)
    z = xn @ w_in
    sizes = (ATTN_WIDTH, ATTN_WIDTH, ATTN_WIDTH, IDX_HEADS * IDX_DIM, IDX_DIM, IDX_HEADS,
             2 * CONV_CH, D_MODEL, D_MODEL)
    q, k, v, iq, ik, iw, cz, ga, gb = jnp.split(z, np.cumsum(sizes)[:-1].tolist(), axis=-1)
    q = rmsnorm(q.reshape(B, T, N_HEADS, HEAD_DIM), q_g)
    k = rmsnorm(k.reshape(B, T, N_HEADS, HEAD_DIM), k_g)
    v = v.reshape(B, T, N_HEADS, HEAD_DIM)
    iq = iq.reshape(B, T, IDX_HEADS, IDX_DIM)
    u = cz[..., :CONV_CH] * jax.nn.sigmoid(cz[..., CONV_CH:])
    return q, k, v, iq, ik, iw, u, ga, gb

def conv_branch(u, ctx, w_dw, b_dw, ln_g, ln_b, w_b):
    full = jnp.concatenate([ctx.astype(u.dtype), u], axis=1)
    y = lax.conv_general_dilated(full, w_dw[:, None, :], window_strides=(1,), padding='VALID',
                                 dimension_numbers=('NWC', 'WIO', 'NWC'),
                                 feature_group_count=CONV_CH) + b_dw
    y = jax.nn.silu(layernorm(y, ln_g, ln_b))
    return y @ w_b, full[:, -CONV_CTX:]

def merge_and_ffn(x, attn_o, conv_o, ga, gb, w_a, w_out, g_ffn, w_gate, w_up, w_down):
    B, T = x.shape[0], x.shape[1]
    a = attn_o.reshape(B, T, ATTN_WIDTH) @ w_a
    m = jax.nn.sigmoid(ga) * a + jax.nn.sigmoid(gb) * conv_o
    h = x + m @ w_out
    hn = rmsnorm(h, g_ffn)
    return h + (jax.nn.silu(hn @ w_gate) * (hn @ w_up)) @ w_down

def prompt_attention(q, k, v, iq, iw, ik, rel_bias):
    B, T = q.shape[0], q.shape[1]
    n_blk = -(-T // Q_BLOCK)
    pad = n_blk * Q_BLOCK - T
    top_k = min(TOPK_MAX, SEQ // 4)
    k_pos = jnp.arange(T, dtype=jnp.int32)

    def blocks(a):
        a = jnp.pad(a, [(0, 0), (0, pad)] + [(0, 0)] * (a.ndim - 2))
        return jnp.moveaxis(a.reshape((B, n_blk, Q_BLOCK) + a.shape[2:]), 1, 0)

    q_pos_b = jnp.arange(n_blk * Q_BLOCK, dtype=jnp.int32).reshape(n_blk, Q_BLOCK)

    def one_block(args):
        qb, iqb, iwb, qp = args
        s = index_scores(iqb, iwb, ik, qp, k_pos)
        _, sel = lax.top_k(s, top_k)
        return sparse_attend(qb, take_rows(k, sel), take_rows(v, sel), qp, sel, rel_bias)

    o = lax.map(one_block, (blocks(q), blocks(iq), blocks(iw), q_pos_b))
    return jnp.moveaxis(o, 0, 1).reshape(B, n_blk * Q_BLOCK, N_HEADS, HEAD_DIM)[:, :T]

def sample_attention(q, k_new, v_new, iq, iw, ik_new, cache_k, cache_v, cache_ik, page_table, rel_bias):
    B, Q = q.shape[0], q.shape[1]
    L = PAST_LEN + Q
    top_k = min(TOPK_MAX, L // 4)
    ik_past = cache_ik[page_table].reshape(B, PAST_LEN, IDX_DIM)
    ik_all = jnp.concatenate([ik_past.astype(ik_new.dtype), ik_new], axis=1)
    q_pos = PAST_LEN + jnp.arange(Q, dtype=jnp.int32)
    s = index_scores(iq, iw, ik_all, q_pos, jnp.arange(L, dtype=jnp.int32))
    _, sel = lax.top_k(s, top_k)
    in_past = (sel < PAST_LEN)[..., None, None]
    ps = jnp.minimum(sel, PAST_LEN - 1)
    phys = take_rows(page_table, ps // PAGE_SIZE)
    slot = ps % PAGE_SIZE
    ns = jnp.clip(sel - PAST_LEN, 0, Q - 1)
    k_sel = jnp.where(in_past, cache_k[phys, slot].astype(k_new.dtype), take_rows(k_new, ns))
    v_sel = jnp.where(in_past, cache_v[phys, slot].astype(v_new.dtype), take_rows(v_new, ns))
    return sparse_attend(q, k_sel, v_sel, q_pos, sel, rel_bias)

def setup_inputs(seed: int = 0) -> dict:
    key = jax.random.key(seed)
    ks = jax.random.split(key, 26)
    n_pages = PAST_LEN // PAGE_SIZE
    n_used = DEC_BATCH * n_pages
    n_pool = (n_used * 5) // 4

    def nrm(k, shape, scale):
        return jax.random.normal(k, shape, jnp.float32) * scale

    def gain(k, shape):
        return 1.0 + 0.01 * jax.random.normal(k, shape, jnp.float32)

    page_table = jax.random.permutation(ks[6], n_pool)[:n_used].reshape(DEC_BATCH, n_pages).astype(jnp.int32)
    return {
        'x_prompt': nrm(ks[0], (BATCH, SEQ, D_MODEL), 1.0),
        'x_sample': nrm(ks[1], (DEC_BATCH, DEC_SEQ, D_MODEL), 1.0),
        'cache_k': nrm(ks[2], (DEPTH, n_pool, PAGE_SIZE, N_HEADS, HEAD_DIM), 1.0),
        'cache_v': nrm(ks[3], (DEPTH, n_pool, PAGE_SIZE, N_HEADS, HEAD_DIM), 1.0),
        'cache_ik': nrm(ks[4], (DEPTH, n_pool, PAGE_SIZE, IDX_DIM), 1.0),
        'state_conv': nrm(ks[5], (DEPTH, DEC_BATCH, CONV_CTX, CONV_CH), 0.5),
        'page_table': page_table,
        'meta_tokens': nrm(ks[7], (N_META, D_MODEL), 1.0),
        'rel_bias': nrm(ks[8], (REL_BUCKETS, N_HEADS), 0.5),
        'norm_mix_g': gain(ks[9], (DEPTH, D_MODEL)),
        'w_in': nrm(ks[10], (DEPTH, D_MODEL, D_IN), D_MODEL ** -0.5),
        'q_norm_g': gain(ks[11], (DEPTH, HEAD_DIM)),
        'k_norm_g': gain(ks[12], (DEPTH, HEAD_DIM)),
        'w_attn_br': nrm(ks[13], (DEPTH, ATTN_WIDTH, D_MODEL), ATTN_WIDTH ** -0.5),
        'w_dw': nrm(ks[14], (DEPTH, CONV_WIDTH, CONV_CH), CONV_WIDTH ** -0.5),
        'b_dw': nrm(ks[15], (DEPTH, CONV_CH), 0.01),
        'ln_conv_g': gain(ks[16], (DEPTH, CONV_CH)),
        'ln_conv_b': nrm(ks[17], (DEPTH, CONV_CH), 0.01),
        'w_conv_br': nrm(ks[18], (DEPTH, CONV_CH, D_MODEL), CONV_CH ** -0.5),
        'w_out': nrm(ks[19], (DEPTH, D_MODEL, D_MODEL), D_MODEL ** -0.5),
        'norm_ffn_g': gain(ks[20], (DEPTH, D_MODEL)),
        'w_ffn_gate': nrm(ks[21], (DEPTH, D_MODEL, D_FF), D_MODEL ** -0.5),
        'w_ffn_up': nrm(ks[22], (DEPTH, D_MODEL, D_FF), D_MODEL ** -0.5),
        'w_ffn_down': nrm(ks[23], (DEPTH, D_FF, D_MODEL), D_FF ** -0.5),
    }

def reference(x_prompt, x_sample, cache_k, cache_v, cache_ik, state_conv, page_table,
              meta_tokens, rel_bias, norm_mix_g, w_in, q_norm_g, k_norm_g, w_attn_br,
              w_dw, b_dw, ln_conv_g, ln_conv_b, w_conv_br, w_out, norm_ffn_g,
              w_ffn_gate, w_ffn_up, w_ffn_down):
    B = x_prompt.shape[0]
    hp = jnp.concatenate([jnp.broadcast_to(meta_tokens[None].astype(x_prompt.dtype),
                                           (B, N_META, D_MODEL)), x_prompt], axis=1)
    hs = x_sample
    kp_l, vp_l, ikp_l, cp_l = [], [], [], []
    ks_l, vs_l, iks_l, cs_l = [], [], [], []
    for l in range(DEPTH):
        q, k, v, iq, ik, iw, u, ga, gb = mixer_inputs(hp, norm_mix_g[l], w_in[l], q_norm_g[l], k_norm_g[l])
        ao = prompt_attention(q, k, v, iq, iw, ik, rel_bias)
        ctx0 = jnp.zeros((B, CONV_CTX, CONV_CH), u.dtype)
        co, cst = conv_branch(u, ctx0, w_dw[l], b_dw[l], ln_conv_g[l], ln_conv_b[l], w_conv_br[l])
        hp = merge_and_ffn(hp, ao, co, ga, gb, w_attn_br[l], w_out[l], norm_ffn_g[l],
                           w_ffn_gate[l], w_ffn_up[l], w_ffn_down[l])
        kp_l.append(k); vp_l.append(v); ikp_l.append(ik); cp_l.append(cst)
        q, k, v, iq, ik, iw, u, ga, gb = mixer_inputs(hs, norm_mix_g[l], w_in[l], q_norm_g[l], k_norm_g[l])
        ao = sample_attention(q, k, v, iq, iw, ik, cache_k[l], cache_v[l], cache_ik[l], page_table, rel_bias)
        co, cst = conv_branch(u, state_conv[l], w_dw[l], b_dw[l], ln_conv_g[l], ln_conv_b[l], w_conv_br[l])
        hs = merge_and_ffn(hs, ao, co, ga, gb, w_attn_br[l], w_out[l], norm_ffn_g[l],
                           w_ffn_gate[l], w_ffn_up[l], w_ffn_down[l])
        ks_l.append(k); vs_l.append(v); iks_l.append(ik); cs_l.append(cst)
    return (hp[:, N_META:], hs,
            jnp.stack(kp_l), jnp.stack(vp_l), jnp.stack(ikp_l), jnp.stack(cp_l),
            jnp.stack(ks_l), jnp.stack(vs_l), jnp.stack(iks_l), jnp.stack(cs_l))


_drawn_inputs = setup_inputs


def setup_inputs(seed=0):
    import zlib

    import numpy as np

    out = dict(_drawn_inputs(seed))
    spreads = {}
    factors = {'norm_mix_g': 4.316,
     'q_norm_g': 8.0,
     'k_norm_g': 6.082,
     'b_dw': 7.981,
     'ln_conv_g': 8.0,
     'ln_conv_b': 8.0,
     'norm_ffn_g': 8.0}
    for name, (base, spread) in spreads.items():
        noise = np.random.default_rng([zlib.crc32(name.encode()), seed]).standard_normal(out[name].shape)
        drawn = base * np.exp(spread * noise) if base else spread * noise
        out[name] = __import__('jax').numpy.asarray(drawn.astype(out[name].dtype))
    for name, factor in factors.items():
        out[name] = (out[name] * factor).astype(out[name].dtype)
    return out
```

```python
from contextlib import ExitStack

import concourse.bass as bass
from concourse import mybir

F32 = mybir.dt.float32
F32R = mybir.dt.float32r
I32 = mybir.dt.int32
ALU = mybir.AluOpType
ACT = mybir.ActivationFunctionType
AX = mybir.AxisListType.X

P = 128
D = 2048
KT = D // P
N_META, SEQ, B, Q = 16, 256, 8, 8
NS = B * Q
NP = N_META + SEQ
NT = NP + NS
NQ = SEQ + NS
T0C = N_META
H = 8
IH, ID = 16, 64
PAST, PAGE = 1024, 128
NPG = PAST // PAGE
LS = PAST + Q
TOPK_P, TOPK_S = SEQ // 4, 256
CC, CW = 1024, 31
CT = CC // P
CTX = CW - 1
FF = 5632
EPS = 1e-6
NEG = -1e30
OUT_OF_REACH = -3.0e38
TAKEN = -3.4e38
BUCKETS, MAX_DIST = 32, 128

C_Q, C_K, C_V = 0, 1024, 2048
C_IQ, C_IK, C_IW = 3072, 4096, 4160
C_CZ = 4176
C_GA = C_CZ + 2 * CC
C_GB = C_GA + D

UP = N_META - 2 + NP
UPAD = CTX - N_META
UW = UP + B * (CTX + Q)
RELW = 400

OH_G, OH_T7, OH_NEW, OH_FAR, OH_N = 0, RELW, RELW + Q * P, RELW + Q * P + Q * NS, RELW + Q * P + Q * NS + P

R_GMIX, R_GFFN, R_BDW, R_LNG, R_LNB, R_QG, R_KG, R_N = 0, 16, 32, 40, 48, 56, 57, 58


class Chain:

    def __init__(self, eng, sem):
        self.eng, self.sem, self.start, self.g, self.per, self.k = eng, sem, 0, 0, 0, 0

    def loop(self, g, per):
        self.g, self.per, self.k = g, per, 0

    def end(self, n):
        assert self.k == self.per, (self.k, self.per)
        self.start += n * self.per
        self.g = self.per = self.k = 0

    def value(self):
        return self.start + self.g * self.per + self.k if self.per else self.start

    def step(self, ins):
        ins.then_inc(self.sem, 1)
        if self.per:
            self.k += 1
        else:
            self.start += 1

    def wait(self):
        self.eng.wait_ge(self.sem, self.value())

    def rest(self):
        self.wait()
        self.eng.memset(self.spare, 0.0)

    def wait_back(self, n):
        self.eng.wait_ge(self.sem, self.value() - n)

    def link(self, ins):
        self.step(ins)
        self.wait()


def loop(eng, n, body):
    if n == 1:
        body(0)
    else:
        with eng.Fori(0, n) as g:
            body(g)



def place(persistent, transient):
    def size(shape):
        n = 4
        for x in shape[1:]:
            n *= x
        return (n + 31) // 32 * 32

    top, where = 16512, {}
    for name, shape, _ in persistent:
        where[name] = top
        top += size(shape)
    base, placed = top, []
    for name, shape, _, first, last in sorted(transient, key=lambda t: PLACING.index(t[0])):
        off = base
        for o, n, f, l in sorted(placed):
            if f <= last and first <= l and o < off + size(shape) and off < o + n:
                off = o + n
        assert off + size(shape) <= 229344, (name, off, size(shape))
        placed.append((off, size(shape), first, last))
        where[name] = off
    return where


(ST_A, ST_IQ, ST_IKIW, ST_INDEX, ST_QK, ST_V, ST_PROMPT, ST_KOUT, ST_CZ, ST_SOFTMAX, ST_GA, ST_OSPLIT, ST_NORM,
 ST_MERGE, ST_OUT, ST_FFN) = range(16)

PERSISTENT = [
    ("XH", [P, KT, NT], F32R), ("XL", [P, KT, NT], F32R),
    ("RAW", [P, 4, KT, P], F32), ("WH", [P, 2, KT, P], F32R), ("WL", [P, 2, KT, P], F32R),
    ("ident", [P, P], F32), ("ones", [P, P], F32), ("zer", [P, P], F32),
    ("prm", [P, R_N], F32), ("gqk", [P, 2 * H], F32), ("wdw", [P, CT, CW], F32),
    ("eps", [P, 1], F32), ("stat", [P, 64], F32), ("ptab", [1, B * NPG], I32),
    ("biasS", [P, NPG, H, Q], F32), ("biasN", [NS, H, Q], F32),
]
TRANSIENT = [
    ("hT", [P, KT, NQ], F32, ST_OUT, ST_FFN),
    ("SGA", [P, KT, NQ], F32, ST_GA, ST_FFN),
    ("ML", [P, KT, NQ], F32R, ST_MERGE, ST_FFN),
    ("OH", [P, H, NQ], F32R, ST_OSPLIT, ST_MERGE), ("OL", [P, H, NQ], F32R, ST_OSPLIT, ST_MERGE),
    ("ub", [P, CT, UW], F32, ST_KOUT, ST_NORM),
    ("oT", [P, H, NQ], F32, ST_PROMPT, ST_OSPLIT),
    ("vs", [NS, CC], F32, ST_V, ST_OSPLIT),
    ("LN", [NS, B, H, Q], F32, ST_KOUT, ST_OSPLIT), ("rS", [P, B, H, Q], F32, ST_SOFTMAX, ST_OSPLIT),
    ("Ss", [NS, LS], F32, ST_INDEX, ST_SOFTMAX), ("Ws", [NS, LS], F32, ST_INDEX, ST_SOFTMAX),
    ("m8s", [NS, 8], F32, ST_INDEX, ST_CZ),
    ("L", [P, NPG, B, H * Q], F32, ST_CZ, ST_GA), ("ya", [P, 2, 2, NQ], F32, ST_GA, ST_GA),
    ("Sp", [P, 2, NP], F32, ST_INDEX, ST_PROMPT), ("Wp", [P, 2, NP], F32, ST_INDEX, ST_PROMPT),
    ("m8p", [P, 2, 8], F32, ST_INDEX, ST_QK),
    ("CH", [P, CT, NQ], F32R, ST_NORM, ST_MERGE), ("CL", [P, CT, NQ], F32R, ST_NORM, ST_MERGE),
    ("xtok", [P, 3, D], F32, ST_A, ST_A), ("xs", [P, 3, D], F32, ST_A, ST_A),
    ("xTs", [P, KT, NQ], F32, ST_A, ST_A), 
    ("oh", [33, OH_N], F32, ST_A, ST_A), ("wrow", [CW, CC], F32, ST_A, ST_A),
    ("prow", [R_N, P], F32, ST_A, ST_A), ("relx", [33, H], F32, ST_A, ST_A),
    ("gsb", [H, RELW], F32, ST_A, ST_A),
    ("esel", [IH, P], F32, ST_A, ST_INDEX), ("qm", [P, Q], F32, ST_A, ST_INDEX),
    ("cms", [NS, Q], F32, ST_A, ST_INDEX), ("cmp", [P, 2, NP], F32, ST_A, ST_INDEX),
    ("ikst", [P, B, NPG, ID], F32, ST_IQ, ST_INDEX),
    ("iqT", [P, H, SEQ], F32, ST_IQ, ST_INDEX), ("iqs", [P, B, H, 2, Q], F32, ST_IQ, ST_INDEX),
    ("ikT", [P, NT], F32, ST_IKIW, ST_INDEX), ("iwT", [IH, NT], F32, ST_IKIW, ST_INDEX),
    ("IW", [P, B, NS + Q], F32, ST_IKIW, ST_INDEX), ("iktok", [P, 3, ID], F32, ST_INDEX, ST_QK),
    ("iwtok", [P, 2, IH], F32, ST_INDEX, ST_INDEX),
    ("iqb", [P, 2, P], F32, ST_INDEX, ST_INDEX), ("iwb", [P, 2, NS], F32, ST_INDEX, ST_INDEX),
    ("ikb", [P, 2, NPG, 2, ID], F32, ST_INDEX, ST_INDEX), ("ikTp", [P, 2, PAST], F32, ST_INDEX, ST_INDEX),
    ("rl", [P, 2, LS], F32, ST_INDEX, ST_INDEX), ("rp", [P, 2, NP], F32, ST_INDEX, ST_INDEX),
    ("QK", [P, 2 * H, NT], F32, ST_QK, ST_KOUT),
    ("sq", [P, 2, NT], F32, ST_QK, ST_QK), ("rt", [P, 2, NT], F32, ST_QK, ST_QK),
    ("vT", [P, 2, NT], F32, ST_V, ST_V), ("vtok", [P, 2, CC], F32, ST_V, ST_KOUT),
    ("v2", [16, CC], F32, ST_V, ST_KOUT), ("Tb", [P, H, NP], F32, ST_V, ST_PROMPT),
    ("sct", [120, 2, CC], F32, ST_KOUT, ST_KOUT),
    ("Lp", [P, 2, NP], F32, ST_PROMPT, ST_PROMPT), ("pT", [P, 2, 3, P], F32, ST_PROMPT, ST_PROMPT),
    ("ktok", [P, 2, 3, P], F32, ST_KOUT, ST_KOUT), ("qs", [P, H, NS], F32, ST_KOUT, ST_CZ),
    ("kst", [P, 4, CC], F32, ST_CZ, ST_CZ), ("kTs", [P, H, P], F32, ST_CZ, ST_CZ),
    ("sgt", [P, NT], F32, ST_CZ, ST_CZ), ("cblk", [NS, NS], F32, ST_CZ, ST_SOFTMAX),
    ("crp", [Q, NS], F32, ST_CZ, ST_SOFTMAX), ("vst", [P, 4, CC], F32, ST_GA, ST_GA),
    ("MS", [P, NPG, NS], F32, ST_SOFTMAX, ST_SOFTMAX), ("MN", [NS, NS], F32, ST_SOFTMAX, ST_SOFTMAX),
    ("e8", [Q, NS], F32, ST_SOFTMAX, ST_SOFTMAX), ("mx", [P, 4, P], F32, ST_SOFTMAX, ST_SOFTMAX),
    ("dg", [P, 4, P], F32, ST_SOFTMAX, ST_SOFTMAX), ("utok", [32, CC], F32, ST_SOFTMAX, ST_SOFTMAX), ("uss", [P, CT, B, Q], F32, ST_SOFTMAX, ST_SOFTMAX),
    ("ustok", [NS, CC], F32, ST_SOFTMAX, ST_SOFTMAX),
    ("csq", [P, 2, NQ], F32, ST_NORM, ST_NORM),
    ("crt", [P, NQ], F32, ST_NORM, ST_NORM),
    ("gbs", [P, 2, NQ], F32, ST_MERGE, ST_MERGE), ("mt", [P, 2, NQ], F32, ST_MERGE, ST_MERGE),
    ("mu_", [P, NQ], F32, ST_MERGE, ST_MERGE),
    ("sq2", [P, 2, NQ], F32, ST_OUT, ST_OUT), ("rf", [P, NQ], F32, ST_OUT, ST_FFN),
    ("gt", [P, 2, NQ], F32, ST_FFN, ST_FFN), ("ut", [P, NQ], F32, ST_FFN, ST_FFN),
    ("at", [P, 2, NQ], F32, ST_FFN, ST_FFN), ("ytok", [P, 4, 3, P], F32, ST_FFN, ST_FFN),
]
PLACING = ("hT ikst vst qm pT utok iqs ML L wrow crp QK OH ub vs rp Ss esel OL dg ya rS sq2 oT qs sgt IW oh mt m8s "
           "ytok LN kst prow iwT crt ikTp xTs rt Ws ikT iqT xs rl cms cmp relx iwtok CH iwb MN xtok mx iqb Wp sq m8p "
           "uss gt Sp vT kTs vtok sct Tb ustok Lp gsb SGA MS e8 gbs rf cblk CL ikb v2 mu_ iktok csq ktok ut at ").split()


def layer(nc, I, O):
    gscr = nc.dram_tensor("bias_scratch", (H, P, RELW), F32)
    xscr = nc.dram_tensor("xT_scratch", (D, NQ), F32).ap()

    def tiles(w):
        return w[0].rearrange("(k p) n -> p k n", p=P)

    w_in, w_a, w_c, w_o = tiles(I["w_in"]), tiles(I["w_attn_br"]), tiles(I["w_conv_br"]), tiles(I["w_out"])
    w_g, w_u, w_d = tiles(I["w_ffn_gate"]), tiles(I["w_ffn_up"]), tiles(I["w_ffn_down"])
    cache_k = I["cache_k"][0].rearrange("g s h d -> g s (h d)")
    cache_v = I["cache_v"][0].rearrange("g s h d -> g s (h d)")
    cache_ik = I["cache_ik"][0]
    POOL_PAGES = cache_ik.shape[0]

    PARTS = [(0, 16), (16, 16), (32, 12)]
    assert sum(m for _, m in PARTS) * P == FF
    plan = [("iq", 8), ("ikiw", 4), ("qk", 16), ("v", 8), ("cz", 16), ("ga", 16), ("merge", 32), ("out", 16)]
    for n, (_, m) in enumerate(PARTS):
        plan += [(f"gu{n}", 2 * m), (f"dn{n}", 16)]
    G0, GN, at = {}, {}, 0
    for name, n in plan:
        assert n % 4 == 0
        G0[name], GN[name] = at, n // 4
        at += n // 4
    GROUPS = at

    where = place(PERSISTENT, TRANSIENT)
    T = {}
    for name, shape, dt, *_ in PERSISTENT + TRANSIENT:
        T[name] = nc.alloc_sbuf_tensor_at(name, shape, dt, offset=where[name])
    T["MH"] = nc.alloc_sbuf_tensor_at("MH", [P, KT, NQ], F32R, offset=where["SGA"])

    XH, XL, RAW, WH, WL = T["XH"], T["XL"], T["RAW"], T["WH"], T["WL"]
    ident, ones, zer, prm, gqk, wdw, eps, stat = (T[x] for x in ("ident", "ones", "zer", "prm", "gqk", "wdw", "eps", "stat"))
    ptab, biasS, biasN = T["ptab"], T["biasS"], T["biasN"]
    hT, SGA, MH, ML, OH, OL, CH, CL = (T[x] for x in ("hT", "SGA", "MH", "ML", "OH", "OL", "CH", "CL"))
    ub, oT, vs, LN, rS, Ss, Ws, L, Sp, Wp = (T[x] for x in ("ub", "oT", "vs", "LN", "rS", "Ss", "Ws", "L", "Sp", "Wp"))
    m8s, m8p = T["m8s"], T["m8p"]
    xtok, xs, xTs, oh, wrow, prow, relx, gsb = (T[x] for x in ("xtok", "xs", "xTs", "oh", "wrow", "prow", "relx", "gsb"))
    esel, qm, cms, cmp_, ikst, iqT, iqs, ikT, iwT, IW = (T[x] for x in ("esel", "qm", "cms", "cmp", "ikst", "iqT", "iqs", "ikT", "iwT", "IW"))
    iktok, iwtok, iqb, iwb, ikb, ikTp, rl, rp = (T[x] for x in ("iktok", "iwtok", "iqb", "iwb", "ikb", "ikTp", "rl", "rp"))
    QK, sq, rt, vT, vtok, v2, Tb, sct, Lp, pT, ktok, qs = (T[x] for x in ("QK", "sq", "rt", "vT", "vtok", "v2", "Tb", "sct", "Lp", "pT", "ktok", "qs"))
    kst, kTs, sgt, cblk, crp, vst, MS, MN, e8, mx, dg = (T[x] for x in ("kst", "kTs", "sgt", "cblk", "crp", "vst", "MS", "MN", "e8", "mx", "dg"))
    uss = T["uss"]
    utok, ustok, ya, csq, crt, gbs, mt, mu_, sq2, rf, gt, ut, at2, ytok = (
        T[x] for x in ("utok", "ustok", "ya", "csq", "crt", "gbs", "mt", "mu_", "sq2", "rf", "gt", "ut", "at", "ytok"))

    XTILES = [(0, P), (P, P), (2 * P, NT - 2 * P)]
    QTILES = [(0, P), (P, P), (2 * P, NS)]

    def keys_of(qt):
        return N_META + P * (qt + 1)

    with ExitStack() as ctx:
        G, TB, SB, MB = ([ctx.enter_context(nc.psum_tensor(f"ps{n}{i}", [P, 512], F32)) for i in range(2)] for n in "GTSM")

        def sem(name):
            return ctx.enter_context(nc.semaphore(name))

        def sems(name, n):
            return [sem(f"{name}{i}") for i in range(n)]

        w_ld = sems("w_ld", 4)
        hi_done, lo_done, mm_done = sem("hi_done"), sem("lo_done"), sem("mm_done")
        ev = sems("ev", 2)
        x_ld, c_ld, c2_ld, g_wr, x_wr, tb_ld = sem("x_ld"), sem("c_ld"), sem("c2_ld"), sem("g_wr"), sem("x_wr"), sem("tb_ld")
        pool_init, pool_zero = sem("pool_init"), sem("pool_zero")
        a_par, a_prm, a_tab, a_bias, a_sqrt, a_xs, a_tr = sem("a_par"), sem("a_prm"), sem("a_tab"), sem("a_bias"), sem("a_sqrt"), sem("a_xs"), sem("a_tr")
        a_hi, a_lo, a_rawA, a_rawD = sem("a_hi"), sem("a_lo"), sem("a_rawA"), sem("a_rawD")
        act_ch, dve_ch = sem("act_ch"), sem("dve_ch")
        ik_ld, d_setup, d_iw, d_stage, ik_tr = sem("ik_ld"), sem("d_setup"), sem("d_iw"), sem("d_stage"), sem("ik_tr")
        d_cpA, d_cpD, idx_mm, d_rlA, d_rlD, sum_mm, d_ss = sem("d_cpA"), sem("d_cpD"), sem("idx_mm"), sem("d_rlA"), sem("d_rlD"), sem("sum_mm"), sem("d_ss")
        pp_mm, pp_relu, pp_acc, o_ik = sem("pp_mm"), sem("pp_relu"), sem("pp_acc"), sem("o_ik")
        sq_done, st_done, sqrt_done, nm_done, vtr, vk_done = sem("sq_done"), sem("st_done"), sem("sqrt_done"), sem("nm_done"), sem("vtr"), sem("vk_done")
        p_qk, p_lg, p_max, p_exp, p_nrm, p_tr, p_cp, p_pv, p_o = (sem(x) for x in ("p_qk", "p_lg", "p_max", "p_exp", "p_nrm", "p_tr", "p_cp", "p_pv", "p_o"))
        ko_tr, ko_cp, ko_wr, v_wr, ln_mm, ln_dn, qs_dn = sem("ko_tr"), sem("ko_cp"), sems("ko_wr", 2), sem("v_wr"), sem("ln_mm"), sem("ln_dn"), sem("qs_dn")
        sc_ld, sc_tr, sc_cp, ub_z, cs_wr = sem("sc_ld"), sem("sc_tr"), sem("sc_cp"), sem("ub_z"), sem("cs_wr")
        k_ld, k_tr, kc_A, kc_D, kq_done, lg_done = sems("k_ld", 4), sem("k_tr"), sem("kc_A"), sem("kc_D"), sem("kq_done"), sem("lg_done")
        cb_ld, u_s, u_tr, u_cp, u_wr = sem("cb_ld"), sem("u_s"), sem("u_tr"), sem("u_cp"), sem("u_wr")
        x_e, x_tr, x_m, x_rep, x_mn, x_mx, x_mt, x_dg, x_bc, x_sub, x_exp, x_sm, x_den, x_rs = (
            sem(f"x_{n}") for n in ("e", "tr", "m", "rep", "mn", "mx", "mt", "dg", "bc", "sub", "exp", "sm", "den", "rs"))
        v_ld, v_used, os_done, cv_done, yc_done = sems("v_ld", 4), sem("v_used"), sem("os_done"), sem("cv_done"), sem("yc_done")
        np_mm, o_sc, oh_dn, ol_dn, mu_mm, mu_dn, cs_sq, va_mm, cs_rt, cy_dn, cs_si, ch_dn, cl_dn = (
            sem(x) for x in ("np_mm", "o_sc", "oh_dn", "ol_dn", "mu_mm", "mu_dn", "cs_sq", "va_mm", "cs_rt", "cy_dn", "cs_si", "ch_dn", "cl_dn"))
        m_dn, mh_dn, ml_dn = sem("m_dn"), sem("mh_dn"), sem("ml_dn")
        h_ld = sems("h_ld", 2)
        h_sq, h_st, xh_dn, xl_dn, rf_sq, rf_dn = (sem(x) for x in ( "h_sq", "h_st", "xh_dn", "xl_dn", "rf_sq", "rf_dn"))
        si_dn, ac_dn, ah_dn, al_dn, y_tr, y_cp = (sem(x) for x in ("si_dn", "ac_dn", "ah_dn", "al_dn", "y_tr", "y_cp"))
        y_wr = sems("y_wr", 4)

        block = ctx.enter_context(nc.Block())

        @block.sync
        def _(sp):
            sp.dma_start(xtok[0:N_META, 0, :], I["meta_tokens"]).then_inc(x_ld, 16)
            xp = I["x_prompt"][0]
            sp.dma_start(xtok[N_META:P, 0, :], xp[0:P - N_META]).then_inc(x_ld, 16)
            sp.dma_start(xtok[:, 1, :], xp[P - N_META:2 * P - N_META]).then_inc(x_ld, 16)
            sp.dma_start(xtok[0:N_META, 2, :], xp[2 * P - N_META:SEQ]).then_inc(x_ld, 16)
            sp.dma_start(xtok[N_META:N_META + NS, 2, :], I["x_sample"].rearrange("b q d -> (b q) d")).then_inc(x_ld, 16)

            def load(G_, s, dst_a, src_a, dst_b, src_b, first=False):
                if not first:
                    sp.wait_ge(lo_done, 16 * G_ + (4 * s - 12))
                sp.dma_start(dst_a, src_a).then_inc(w_ld[s], 16)
                sp.dma_start(dst_b, src_b).then_inc(w_ld[s], 16)

            def columns(G_, s, w, col, k0=0, m=KT, first=False):
                c = bass.ds(col if isinstance(col, int) else sp.snap(col), P)
                load(G_, s, RAW[:, s, 0:8, :], w[:, k0:k0 + 8, c], RAW[:, s, 8:m, :], w[:, k0 + 8:k0 + m, c], first)

            for s in range(4):
                columns(0, s, w_in, C_IQ + P * s, first=True)
            for s in range(4):
                columns(1, s, w_in, C_IQ + P * (4 + s))
            for s in range(2):
                w = w_in[:, 8 * s:8 * s + 8, C_IK:C_IK + ID]
                load(G0["ikiw"], s, RAW[:, s, 0:8, 0:ID], w, RAW[:, s, 0:8, ID:P], w)
            for s in range(2):
                w = w_in[:, 8 * s:8 * s + 8, C_IW:C_IW + IH]
                load(G0["ikiw"], 2 + s, RAW[:, 2 + s, 0:4, 0:IH], w[:, 0:4], RAW[:, 2 + s, 4:8, 0:IH], w[:, 4:8])

            def stage(name, unit):
                def body(g):
                    for s in range(4):
                        unit(G0[name] + g, g, s)
                loop(sp, GN[name], body)

            stage("qk", lambda G_, g, s: columns(G_, s, w_in, g * 4 * P + (C_Q + P * s)))
            stage("v", lambda G_, g, s: columns(G_, s, w_in, g * 4 * P + (C_V + P * s)))
            stage("cz", lambda G_, g, s: columns(G_, s, w_in, g * 2 * P + (C_CZ + (CC if s % 2 == 0 else 0) + P * (s // 2))))
            stage("ga", lambda G_, g, s: columns(G_, s, w_in, g * 4 * P + (C_GA + P * s)))

            def merge_unit(G_, g, s):
                if s % 2 == 0:
                    columns(G_, s, w_in, g * 2 * P + (C_GB + P * (s // 2) - 2 * P))
                else:
                    c = bass.ds(g * 2 * P + (P * (s // 2) - 2 * P), P)
                    load(G_, s, RAW[:, s, 0:8, :], w_a[:, :, c], RAW[:, s, 8:16, :], w_c[:, :, c])

            with sp.Fori(1, GN["merge"] + 1) as g:
                for s in range(4):
                    merge_unit(g + (G0["merge"] - 1), g, s)
            stage("out", lambda G_, g, s: columns(G_, s, w_o, g * 4 * P + P * s))
            for n, (k0, m) in enumerate(PARTS):
                stage(f"gu{n}", lambda G_, g, s: columns(G_, s, w_u if s % 2 else w_g, g * 2 * P + P * (k0 + s // 2)))
                stage(f"dn{n}", lambda G_, g, s: columns(G_, s, w_d, g * 4 * P + P * s, k0, m))

        @block.gpsimd
        def _(pool):
            pool.memset(ones[:], 1.0)
            pool.memset(zer[:], 0.0)
            pool.memset(eps[:], EPS)
            pool.memset(stat[:], 1.0).then_inc(pool_init, 1)
            pool.wait_ge(pool_init, 1)
            pool.memset(relx[32:33, :], NEG).then_inc(pool_init, 1)
            pool.sem_inc(ev[0], 1)
            pool.sem_inc(ev[1], 1)
            small = [(ident[:], I["c_ident"]), (oh[:], I["c_oh"]), (relx[0:BUCKETS, :], I["rel_bias"]),
                     (wrow[:], I["w_dw"][0])]
            for r, name, n in ((R_GMIX, "norm_mix_g", KT), (R_GFFN, "norm_ffn_g", KT), (R_BDW, "b_dw", CT), (R_LNG, "ln_conv_g", CT),
                               (R_LNB, "ln_conv_b", CT), (R_QG, "q_norm_g", 1), (R_KG, "k_norm_g", 1)):
                small.append((prow[r:r + n, :], I[name].rearrange("o (n p) -> (o n) p", p=P)))
            assert len(small) == 11
            for dst, src in small:
                pool.dma_start(dst, src).then_inc(c_ld, 16)
            for dst, src in ((ptab[:], I["page_table"].rearrange("b (o n) -> o (b n)", o=1)), (esel[:], I["c_esel"]),
                             (qm[:], I["c_qm"]), (cms[:], I["c_cms"]), (cmp_[:], I["c_cmp"])):
                pool.dma_start(dst, src).then_inc(c2_ld, 16)
            pool.wait_ge(a_bias, 1)
            pool.dma_start(gscr.ap(), gsb[:, None, :].to_broadcast([H, P, RELW])).then_inc(g_wr, 16)
            pool.wait_ge(a_rawA, KT // 2)
            pool.wait_ge(a_rawD, KT // 2)
            pool.dma_start(xscr.rearrange("(k p) n -> p k n", p=P), xTs[:]).then_inc(x_wr, 16)
            pool.wait_ge(g_wr, 16)
            pool.wait_ge(x_wr, 16)
            pool.wait_ge(c2_ld, 80)
            pool.wait_ge(a_lo, KT)
            pool.memset(iqs[:], 0.0)
            pool.memset(IW[:], 0.0).then_inc(pool_zero, 1)

            def page(i):
                return pool.value_load(ptab[0:1, bass.ds(i, 1)], min_val=0, max_val=POOL_PAGES - 1)

            with pool.Fori(0, B) as b:
                for t in range(NPG):
                    pool.dma_start(ikst[:, bass.ds(b, 1), t, :], cache_ik[bass.ds(page(b * NPG + t), 1)].rearrange("o s d -> s o d")).then_inc(ik_ld, 16)
            pool.wait_ge(ik_ld, 16 * B * NPG)
            pool.wait_ge(d_iw, 1)
            pool.wait_ge(d_cpA, 1)
            pool.dma_start(O["ik_prompt"][0, 0, 0:2 * P].rearrange("(i p) d -> p i d", p=P), iktok[:, 0:2, :]).then_inc(o_ik, 16)
            pool.dma_start(O["ik_prompt"][0, 0, 2 * P:NP], iktok[0:NP - 2 * P, 2, :]).then_inc(o_ik, 16)
            pool.dma_start(O["ik_sample"][0].rearrange("b q d -> (b q) d"), iktok[NP - 2 * P:NT - 2 * P, 2, :]).then_inc(o_ik, 16)

            pool.sem_inc(sum_mm, 2)

            def staging(g):
                for j in range(2):
                    b = g * 2 + j
                    pool.wait_ge(sum_mm, b + 1)
                    for r in range(2):
                        pool.tensor_copy(ikb[:, j, :, r, :], ikst[:, bass.ds(b, 1)].rearrange("p o t d -> p (o t) d"))
                    pool.tensor_copy(iqb[:, j:j + 1, :], iqs[:, bass.ds(b, 1)].rearrange("p o h r q -> p o (h r q)"))
                    pool.tensor_copy(iwb[:, j, :], IW[:].rearrange("p b n -> p (b n)")[:, bass.ds(b * NS, NS)]).then_inc(d_stage, 1)

            loop(pool, B // 2, staging)

            pool.wait_ge(nm_done, 2 + 2 * H)
            pool.dma_start(Tb[:], bass.AP(tensor=gscr, offset=P - 1, ap=[[RELW - 1, P], [P * RELW, H], [1, NP]])).then_inc(tb_ld, 16)
            pool.dma_start(O["conv_sample"][0, :, 0:CTX - Q], I["state_conv"][0, :, Q:CTX]).then_inc(cs_wr, 16)
            pool.wait_ge(vk_done, 2 + H)
            vp = O["v_prompt"][0, 0].rearrange("t h d -> t (h d)")
            pool.dma_start(vp[0:2 * P].rearrange("(i p) n -> p i n", p=P), vtok[:]).then_inc(v_wr, 16)
            pool.dma_start(vp[2 * P:NP], v2[:]).then_inc(v_wr, 16)
            pool.dma_start(O["v_sample"][0].rearrange("b q h d -> (b q) (h d)"), vs[:]).then_inc(v_wr, 16)
            pool.wait_ge(p_o, 2 * H)
            for i in range(2):
                pool.dma_start(sct[:, i, :], I["state_conv"][0, 4 * i:4 * i + 4].rearrange("b w c -> (b w) c")).then_inc(sc_ld, 16)
            pool.memset(ub[:, :, 0:UPAD], 0.0).then_inc(ub_z, 1)
            kp = O["k_prompt"][0, 0].rearrange("t h d -> t (h d)")
            ks = O["k_sample"][0].rearrange("b q h d -> (b q) (h d)")
            for h in range(H):
                c = slice(P * h, P * h + P)
                pool.wait_ge(ko_cp, h + 1)
                pool.dma_start(kp[0:2 * P, c].rearrange("(i p) n -> p i n", p=P), ktok[:, h % 2, 0:2, :]).then_inc(ko_wr[h % 2], 16)
                pool.dma_start(kp[2 * P:NP, c], ktok[0:NP - 2 * P, h % 2, 2, :]).then_inc(ko_wr[h % 2], 16)
                pool.dma_start(ks[:, c], ktok[NP - 2 * P:NT - 2 * P, h % 2, 2, :]).then_inc(ko_wr[h % 2], 16)

            pool.wait_ge(v_wr, 48)
            for i in range(2):
                pool.wait_ge(ko_wr[i], 48 * H // 2)
            pool.wait_ge(qs_dn, 1)
            pool.wait_ge(p_o, 2 * H)
            pool.wait_ge(ln_dn, H)
            pool.wait_ge(sc_cp, CT)
            pool.dma_start(cblk[:], I["c_blk"]).then_inc(cb_ld, 16)
            pool.dma_start(crp[:], I["c_rep"]).then_inc(cb_ld, 16)

            def pages(dst, src, landed, used):
                def body(g):
                    for n in range(16):
                        pool.wait_ge(used, g * 16 + (n + 1))
                        pool.dma_start(dst[:, n % 4:n % 4 + 1, :], src[bass.ds(page(g * 16 + n), 1)].rearrange("o s n -> s o n")).then_inc(landed[n % 4], 16)
                return body

            pool.sem_inc(k_tr, 4)
            loop(pool, 4, pages(kst, cache_k, k_ld, k_tr))
            pool.wait_ge(u_cp, 4)
            pool.dma_start(O["conv_prompt"][0, 0], utok[0:CTX, :]).then_inc(u_wr, 16)
            for b in range(B):
                pool.dma_start(O["conv_sample"][0, b, CTX - Q:CTX], ustok[Q * b:Q * b + Q, :]).then_inc(u_wr, 16)
            pool.wait_ge(u_wr, 16 * (1 + B))
            pool.wait_ge(x_rs, 1)
            pool.sem_inc(v_used, 4)
            loop(pool, 4, pages(vst, cache_v, v_ld, v_used))

            pool.wait_ge(ml_dn, KT)
            for i, (a, b) in enumerate([(0, 4), (4, KT)]):
                pool.dma_start(hT[:, a:b, :], xscr.rearrange("(k p) n -> p k n", p=P)[:, a:b, :]).then_inc(h_ld[i], 16)

            yp, ys = O["y_prompt"][0], O["y_sample"].rearrange("b q d -> (b q) d")

            def store(g):
                for s in range(4):
                    c = bass.ds(g * 4 * P + P * s, P)
                    pool.wait_ge(y_cp, g * 4 + (s + 3))
                    pool.dma_start(yp[:, c].rearrange("(i p) n -> p i n", p=P), ytok[:, s, 0:2, :]).then_inc(y_wr[s], 16)
                    pool.dma_start(ys[:, c], ytok[0:NS, s, 2, :]).then_inc(y_wr[s], 16)

            loop(pool, 4, store)
            for s in range(4):
                pool.wait_ge(y_wr[s], 8 * KT)
            pool.wait_ge(o_ik, 48)
            pool.wait_ge(cs_wr, 16)

        @block.scalar
        def _(act):
            ch = Chain(act, act_ch)

            def hi(G_, s, first=False):
                act.wait_ge(w_ld[s], 32 * G_ + 32)
                for r in range(4):
                    quarter(G_, s, r, first)

            def quarter(G_, s, r, first=False):
                if not first:
                    act.wait_ge(mm_done, 16 * G_ + (4 * s + r - 7))
                act.activation(WH[:, s % 2, 4 * r:4 * r + 4], RAW[:, s, 4 * r:4 * r + 4], ACT.Copy).then_inc(hi_done, 1)

            def ahead(G_, s, last=False):
                if not (last and s >= 2):
                    hi(G_ + (s + 2) // 4, (s + 2) % 4)

            def ahead_quarter(G_, s, r):
                G_, s = G_ + (s + 2) // 4, (s + 2) % 4
                if r == 0:
                    act.wait_ge(w_ld[s], 32 * G_ + 32)
                quarter(G_, s, r)

            def done(G_, s):
                act.wait_ge(mm_done, 16 * G_ + (4 * s + 4))

            def ev_wait(G_, s):
                act.wait_ge(ev[s % 2], 2 * G_ + (s // 2 + 2))

            act.wait_ge(x_ld, 80)
            act.wait_ge(pool_init, 2)
            for i, (_, n) in enumerate(XTILES):
                act.activation(xs[0:n, i, :], xtok[0:n, i, :], ACT.Square, accum_out=stat[0:n, i:i + 1]).then_inc(act_ch, 1)
            ch.start += 3
            ch.wait()
            act.activation(stat[:, 4:7], stat[:, 0:3], ACT.Sqrt, scale=1.0 / D, bias=eps[:, 0:1]).then_inc(a_sqrt, 1)
            act.wait_ge(a_prm, 1)
            banks = [TB[0], TB[1], SB[0], SB[1]]
            for k in range(KT):
                act.wait_ge(a_tr, k + 1)
                act.activation(XH[:, k, :], banks[k % 4][:, 0:NT], ACT.Identity, scale=prm[:, R_GMIX + k:R_GMIX + k + 1]).then_inc(a_hi, 1)
            hi(0, 0, True)
            hi(0, 1, True)
            for k in range(0, KT, 2):
                act.wait_ge(a_tr, KT + k + 1)
                act.activation(xTs[:, k, :], banks[k % 4][:, T0C:NT], ACT.Copy).then_inc(a_rawA, 1)

            def iq(g):
                for s in range(4):
                    ahead(G0["iq"] + g, s)
                    done(G0["iq"] + g, s)
                    h = bass.ds(g * 4 + s, 1)
                    act.activation(iqT[:, h, :], G[s % 2][:, None, 0:SEQ], ACT.Copy)
                    for r in range(2):
                        rows = slice(64 * r, 64 * r + 64)
                        ins = act.activation(iqs[rows, :, h, r, :], G[s % 2][rows, SEQ:NQ].rearrange("p (b o q) -> p b o q", b=B, o=1), ACT.Copy)
                    ins.then_inc(ev[s % 2], 1)

            act.wait_ge(pool_zero, 1)
            loop(act, GN["iq"], iq)

            g = G0["ikiw"]
            for s in range(4):
                ahead(g, s)
                if s % 2:
                    done(g, s)
                    half = NT // 2
                    for i in range(2):
                        c = slice(half * i, half * i + half)
                        if s == 1:
                            ins = act.activation(ikT[:, c], MB[0][:, c], ACT.Copy)
                        else:
                            ins = act.activation(iwT[:, c], MB[1][0:IH, c], ACT.Copy, scale=2.0 ** -5)
                        ins.then_inc(ev[i], 1)

            act.wait_ge(d_setup, 1)
            act.activation(iktok[:, 0:2, :], TB[1][:, 0:2 * ID].rearrange("p (i d) -> p i d", i=2), ACT.Copy)
            act.activation(iktok[0:NT - 2 * P, 2, :], TB[1][0:NT - 2 * P, 2 * ID:3 * ID], ACT.Copy).then_inc(d_cpA, 1)
            act.sem_inc(d_rlA, 1)

            def idx(g):
                for j in range(2):
                    b = g * 2 + j
                    act.wait_ge(ik_tr, b + 1)
                    act.activation(ikTp[:, j, 0:512], TB[0][:], ACT.Copy).then_inc(d_cpA, 1)
                    act.wait_ge(idx_mm, b + 1)
                    act.activation(rl[:, j, 0:512], SB[0][:], ACT.Relu)
                    act.activation(rl[:, j, PAST:LS], MB[0][:, 0:Q], ACT.Relu).then_inc(d_rlA, 1)

            loop(act, B // 2, idx)
            for i in range(2 * IH):
                nk = keys_of(i % 2)
                act.wait_ge(pp_mm, i + 1)
                if i >= 2:
                    act.wait_ge(pp_acc, i - 1)
                act.activation(rp[:, i % 2, 0:nk], SB[i % 2][:, 0:nk], ACT.Relu).then_inc(pp_relu, 1)

            act.sem_inc(sqrt_done, 2)

            def qk(g):
                def evacuate(s):
                    done(G0["qk"] + g, s)
                    act.activation(sq[:, s % 2, :], G[s % 2][:, 0:NT], ACT.Square).then_inc(sq_done, 1)
                    act.activation(QK[:, bass.ds(g * 4 + s, 1), :], G[s % 2][:, None, 0:NT], ACT.Copy).then_inc(ev[s % 2], 1)

                def root(s):
                    act.wait_ge(st_done, g * 4 + (s + 1))
                    act.wait_ge(nm_done, g * 4 + (s + 1))
                    act.activation(rt[:, s % 2, :], MB[s % 2][:, 0:NT], ACT.Sqrt, scale=1.0 / P, bias=eps[:, 0:1]).then_inc(sqrt_done, 1)

                for s in range(4):
                    ahead(G0["qk"] + g, s)
                    evacuate(s)
                    if s:
                        root(s - 1)
                root(3)

            loop(act, GN["qk"], qk)

            def v(g):
                for s in range(4):
                    ahead(G0["v"] + g, s)
                    done(G0["v"] + g, s)
                    act.activation(vT[:, s % 2, :], G[s % 2][:, 0:NT], ACT.Copy).then_inc(ev[s % 2], 1)

            act.wait_ge(nm_done, 2 + 2 * H)
            loop(act, GN["v"], v)

            def p_soft(i):
                nk = keys_of(i // H)
                act.wait_ge(p_max, i + 1)
                act.activation(Lp[:, i % 2, 0:nk], Lp[:, i % 2, 0:nk], ACT.Exp, bias=stat[:, 16 + i % 2:17 + i % 2],
                               accum_out=stat[:, 20 + i % 2:21 + i % 2]).then_inc(p_exp, 1)

            p_soft(0)
            for i in range(2 * H):
                if i + 1 < 2 * H:
                    p_soft(i + 1)
                act.wait_ge(p_tr, i + 1)
                if i >= 2:
                    act.wait_ge(p_pv, i - 1)
                full = i // H + 1
                act.activation(pT[:, i % 2, 0:full, :], MB[i % 2][:, 0:full * P].rearrange("p (k n) -> p k n", k=full), ACT.Copy)
                act.activation(pT[0:N_META, i % 2, full, :], MB[i % 2][0:N_META, full * P:full * P + P], ACT.Copy).then_inc(p_cp, 1)
            act.wait_ge(p_o, 2 * H)
            act.activation(qs[:], QK[:, 0:H, NP:NT], ACT.Copy).then_inc(qs_dn, 1)
            for h in range(H):
                act.wait_ge(ko_tr, h + 1)
                if h >= 2:
                    act.wait_ge(ko_wr[h % 2], 48 * (h // 2))
                act.activation(ktok[:, h % 2, 0:2, :], TB[h % 2][:, 0:2 * P].rearrange("p (i d) -> p i d", i=2), ACT.Copy)
                act.activation(ktok[0:NT - 2 * P, h % 2, 2, :], TB[h % 2][0:NT - 2 * P, 2 * P:3 * P], ACT.Copy).then_inc(ko_cp, 1)
            for c in range(CT):
                act.wait_ge(sc_tr, c + 1)
                act.activation(ub[:, c, UP:UW].rearrange("p (b w) -> p b w", b=B)[:, :, 0:CTX],
                               MB[c % 2][:, 0:B * CTX].rearrange("p (b w) -> p b w", b=B), ACT.Copy).then_inc(sc_cp, 1)

            act.sem_inc(kc_A, 1)

            def cz(g):
                for s in range(4):
                    for j in range(4):
                        act.wait_ge(k_tr, g * 16 + (4 * s + j + 5))
                        act.activation(kTs[:, 0:4, :], TB[0][:].rearrange("p (h n) -> p h n", h=4), ACT.Copy).then_inc(kc_A, 1)
                        ahead_quarter(G0["cz"] + g, s, j)
                    if s % 2 == 0:
                        done(G0["cz"] + g, s)
                        act.wait_ge(ev[1], 2 * (G0["cz"] + g) + (1 + s // 2))
                        act.activation(sgt[:], G[0][:, 0:NT], ACT.Sigmoid).then_inc(ev[0], 1)

            loop(act, GN["cz"], cz)

            act.wait_ge(lg_done, B + 2)
            act.activation(uss[:],
                           ub[:, :, UP:UW].rearrange("p c (b w) -> p c b w", b=B)[:, :, :, CTX:CTX + Q], ACT.Copy).then_inc(u_s, 1)
            for i in range(2):
                act.wait_ge(u_tr, i + 1)
                act.activation(utok[0:CTX, 512 * i:512 * i + 512], TB[i][0:CTX, :], ACT.Copy).then_inc(u_cp, 1)
            for i in range(2):
                act.wait_ge(u_tr, i + 3)
                act.activation(ustok[:, 512 * i:512 * i + 512], SB[i][0:NS, :], ACT.Copy).then_inc(u_cp, 1)
            for t in range(NPG):
                act.wait_ge(x_sub, t + 1)
                act.activation(L[:, t], L[:, t], ACT.Exp).then_inc(x_exp, 1)
            act.wait_ge(x_sub, NPG + 1)
            act.activation(LN[:], LN[:], ACT.Exp).then_inc(x_exp, 1)

            act.sem_inc(os_done, 2)
            act.sem_inc(yc_done, 2)

            def ga(g):
                for s in range(4):
                    ahead(G0["ga"] + g, s)
                    done(G0["ga"] + g, s)
                    act.activation(SGA[:, bass.ds(g * 4 + s, 1), :], G[s % 2][:, None, 0:NQ], ACT.Sigmoid).then_inc(ev[s % 2], 1)
                    if s % 2:
                        c = g * 2 + s // 2
                        act.wait_ge(v_used, c * NPG + (NPG + 4))
                        act.activation(oT[:, :, bass.ds(c * Q + SEQ, Q)], SB[s // 2][:, 0:NS].rearrange("p (h q) -> p h q", h=H), ACT.Copy).then_inc(os_done, 1)
                        act.wait_ge(cv_done, c + 1)
                        act.activation(ub[:, bass.ds(c, 1), 0:NQ], ya[:, s // 2, 0:1, :], ACT.Copy).then_inc(yc_done, 1)

            loop(act, GN["ga"], ga)

            act.wait_ge(o_sc, 1)
            act.activation(OH[:], oT[:], ACT.Copy).then_inc(oh_dn, 1)
            for c in range(CT):
                act.wait_ge(mu_dn, c + 1)
                if c >= 2:
                    act.wait_ge(va_mm, c - 1)
                act.activation(csq[:, c % 2, :], ub[:, c, 0:NQ], ACT.Square).then_inc(cs_sq, 1)
            act.wait_ge(va_mm, CT)
            act.activation(crt[:], MB[1][:, 0:NQ], ACT.Sqrt, scale=1.0 / CC, bias=eps[:, 0:1]).then_inc(cs_rt, 1)
            for c in range(CT):
                act.wait_ge(cy_dn, c + 1)
                act.activation(ub[:, c, 0:NQ], ub[:, c, 0:NQ], ACT.Silu, scale=prm[:, R_LNG + c:R_LNG + c + 1],
                               bias=prm[:, R_LNB + c:R_LNB + c + 1]).then_inc(cs_si, 1)
            for c in range(CT):
                act.wait_ge(cs_si, c + 1)
                act.activation(CH[:, c, :], ub[:, c, 0:NQ], ACT.Copy).then_inc(ch_dn, 1)

            def merge(g):
                for s in range(4):
                    ahead(G0["merge"] + g, s)
                    if s % 2 == 0:
                        done(G0["merge"] + g, s)
                        act.activation(gbs[:, s // 2, :], G[0][:, 0:NQ], ACT.Sigmoid).then_inc(ev[0], 1)
                    else:
                        act.wait_ge(m_dn, g * 2 + (s // 2 + 1))
                        act.activation(MH[:, bass.ds(g * 2 + s // 2, 1), :], mt[:, s // 2:s // 2 + 1, :], ACT.Copy).then_inc(mh_dn, 1)

            loop(act, GN["merge"], merge)

            def out(g):
                for s in range(4):
                    ahead(G0["out"] + g, s)
                    f = g * 4 + s
                    ev_wait(G0["out"] + g, s)
                    act.activation(sq2[:, s % 2:s % 2 + 1, :], hT[:, bass.ds(f, 1), :], ACT.Square).then_inc(h_sq, 1)
                    act.activation(XH[:, bass.ds(f, 1), 0:NQ], hT[:, bass.ds(f, 1), :], ACT.Identity,
                                   scale=prm[:, bass.ds(f + R_GFFN, 1)]).then_inc(xh_dn, 1)

            loop(act, GN["out"], out)
            act.wait_ge(h_st, KT + 1)
            act.activation(rf[:], MB[0][:, 0:NQ], ACT.Sqrt, scale=1.0 / D, bias=eps[:, 0:1]).then_inc(rf_sq, 1)

            for n, (k0, m) in enumerate(PARTS):
                def gu(g):
                    for s in range(4):
                        ahead(G0[f"gu{n}"] + g, s)
                        if s % 2 == 0:
                            ev_wait(G0[f"gu{n}"] + g, s)
                            act.activation(gt[:, s // 2, :], gt[:, s // 2, :], ACT.Silu).then_inc(si_dn, 1)
                        else:
                            act.wait_ge(ac_dn, g * 2 + (k0 + s // 2 + 1))
                            act.activation(MH[:, bass.ds(g * 2 + s // 2, 1), :], at2[:, s // 2:s // 2 + 1, :], ACT.Copy).then_inc(ah_dn, 1)

                loop(act, GN[f"gu{n}"], gu)
                final = n == len(PARTS) - 1

                def by_token(g, s):
                    act.wait_ge(y_tr, g * 4 + (s + 1))
                    if not isinstance(g, int) or g:
                        act.wait_ge(y_wr[s], g * 32)
                    act.activation(ytok[:, s, 0:2, :], MB[s % 2][:, 0:2 * P].rearrange("p (i d) -> p i d", i=2), ACT.Copy)
                    act.activation(ytok[0:NS, s, 2, :], MB[s % 2][0:NS, 2 * P:3 * P], ACT.Copy).then_inc(y_cp, 1)

                def dn(g, last=False):
                    for s in range(4):
                        ahead(G0[f"dn{n}"] + g, s, last)
                        if final and s:
                            by_token(g, s - 1)
                    if final:
                        by_token(g, 3)

                if final:
                    act.sem_inc(y_cp, 2)
                    dn(0)
                    with act.Fori(1, GN[f"dn{n}"] - 1) as g:
                        dn(g)
                    dn(GN[f"dn{n}"] - 1, True)
                else:
                    loop(act, GN[f"dn{n}"], dn)

        @block.vector
        def _(dve):
            ch = Chain(dve, dve_ch)
            ch.spare = stat[0:1, 63:64]
            SC = P ** -0.5

            def lo(G_, s):
                for r in range(4):
                    quarter(G_, s, r)

            def quarter(G_, s, r):
                k = slice(4 * r, 4 * r + 4)
                dve.wait_ge(hi_done, 16 * G_ + (4 * s + r + 1))
                dve.tensor_tensor(WL[:, s % 2, k], RAW[:, s, k], WH[:, s % 2, k].bitcast(F32), ALU.subtract).then_inc(lo_done, 1)

            def ahead(G_, s, last=False):
                if not (last and s >= 2):
                    lo(G_ + (s + 2) // 4, (s + 2) % 4)

            def ahead_quarter(G_, s, r):
                quarter(G_ + (s + 2) // 4, (s + 2) % 4, r)

            def done(G_, s):
                dve.wait_ge(mm_done, 16 * G_ + (4 * s + 4))

            def ev_wait(G_, s):
                dve.wait_ge(ev[s % 2], 2 * G_ + (s // 2 + 2))

            dve.wait_ge(a_par, 1)
            ch.step(dve.tensor_copy(prm[:], TB[0][:, 0:R_N]))
            dve.tensor_copy(wdw[:], TB[1][:, 0:CT * CW].rearrange("p (c w) -> p c w", c=CT))
            ch.wait()
            dve.tensor_copy(gqk[:, 0:H], prm[:, R_QG:R_QG + 1].to_broadcast([P, H]))
            dve.tensor_copy(gqk[:, H:2 * H], prm[:, R_KG:R_KG + 1].to_broadcast([P, H])).then_inc(a_prm, 1)
            dve.wait_ge(a_tab, 1)
            dve.tensor_copy(gsb[:], SB[0][0:H, 0:RELW])
            dve.tensor_copy(biasS[:, NPG - 1], SB[1][:, 0:Q * H].rearrange("p (q h) -> p h q", q=Q))
            for t in range(NPG - 1):
                dve.tensor_copy(biasS[:, t], SB[1][:, Q * H:Q * H + H][:, :, None].to_broadcast([P, H, Q]))
            dve.tensor_copy(biasN[:], MB[0][0:NS, 0:Q * H].rearrange("p (q h) -> p h q", q=Q)).then_inc(a_bias, 1)
            dve.wait_ge(a_sqrt, 1)
            ch.link(dve.reciprocal(stat[:, 8:11], stat[:, 4:7]))
            for i, (_, n) in enumerate(XTILES):
                dve.tensor_scalar(xs[0:n, i, :], xtok[0:n, i, :], stat[0:n, 8 + i:9 + i], None, ALU.mult).then_inc(a_xs, 1)
            banks = [TB[0], TB[1], SB[0], SB[1]]
            for k in range(KT):
                dve.wait_ge(a_hi, k + 1)
                dve.scalar_tensor_tensor(XL[:, k, :], banks[k % 4][:, 0:NT], prm[:, R_GMIX + k:R_GMIX + k + 1],
                                         XH[:, k, :].bitcast(F32), ALU.mult, ALU.subtract).then_inc(a_lo, 1)
            lo(0, 0)
            lo(0, 1)
            for k in range(1, KT, 2):
                dve.wait_ge(a_tr, KT + k + 1)
                dve.tensor_copy(xTs[:, k, :], banks[k % 4][:, T0C:NT]).then_inc(a_rawD, 1)

            def ring(name):
                def body(g):
                    for s in range(4):
                        ahead(G0[name] + g, s)
                loop(dve, GN[name], body)

            ring("iq")
            ring("ikiw")

            dve.wait_ge(d_setup, 1)
            dve.tensor_copy(iwtok[:], TB[0][:, 0:2 * IH].rearrange("p (i h) -> p i h", i=2))
            dve.wait_ge(pool_zero, 1)
            dve.tensor_tensor(IW[:, :, 0:Q], TB[0][:, 2 * IH:2 * IH + NS].rearrange("p (b q) -> p b q", b=B),
                              qm[:, None, :].to_broadcast([P, B, Q]), ALU.mult).then_inc(d_iw, 1)
            dve.sem_inc(d_cpD, 1)
            dve.sem_inc(d_rlD, 1)

            def idx(g):
                for j in range(2):
                    b = g * 2 + j
                    dve.wait_ge(ik_tr, b + 1)
                    dve.tensor_copy(ikTp[:, j, 512:PAST], TB[1][:]).then_inc(d_cpD, 1)
                    dve.wait_ge(idx_mm, b + 1)
                    dve.tensor_scalar(rl[:, j, 512:PAST], SB[1][:], 0.0, None, ALU.max).then_inc(d_rlD, 1)

            loop(dve, B // 2, idx)
            dve.wait_ge(sum_mm, B + 3)
            for i in range(2):
                dve.tensor_copy(Ss[:, 512 * i:512 * i + 512], G[i][0:NS, :])
            ch.link(dve.tensor_tensor(Ss[:, PAST:LS], MB[1][0:NS, 0:Q], cms[:], ALU.min))
            dve.tensor_copy(Ws[:], Ss[:]).then_inc(d_ss, 1)
            for i in range(2 * IH):
                h, qt = i // 2, i % 2
                nk = keys_of(qt)
                dve.wait_ge(pp_relu, i + 1)
                if h == 0:
                    ins = dve.tensor_scalar(Sp[:, qt, 0:nk], rp[:, qt, 0:nk], iwtok[:, qt, h:h + 1], None, ALU.mult)
                else:
                    dve.wait_ge(pp_acc, i - 1)
                    ins = dve.scalar_tensor_tensor(Sp[:, qt, 0:nk], rp[:, qt, 0:nk], iwtok[:, qt, h:h + 1], Sp[:, qt, 0:nk],
                                                   ALU.mult, ALU.add)
                ins.then_inc(pp_acc, 1)
            dve.wait_ge(pp_acc, 2 * IH)
            for qt in range(2):
                nk = keys_of(qt)
                ch.link(dve.tensor_tensor(Sp[:, qt, 0:nk], Sp[:, qt, 0:nk], cmp_[:, qt, 0:nk], ALU.min))
                ch.link(dve.tensor_copy(Wp[:, qt, 0:nk], Sp[:, qt, 0:nk]))

            def take8(best, scores):
                best8(best, scores)
                taken8(best, scores)

            def best8(best, scores):
                ch.rest()
                ch.step(dve.max(best, scores))

            def taken8(best, scores):
                ch.rest()
                ch.step(dve.match_replace(scores, best, scores, TAKEN))

            dve.sem_inc(nm_done, 2)

            def qk(g):
                def norm(s):
                    h = bass.ds(g * 4 + s, 1)
                    dve.wait_ge(sqrt_done, g * 4 + (s + 3))
                    ch.link(dve.reciprocal(rt[:, s % 2, :], rt[:, s % 2, :]))
                    dve.scalar_tensor_tensor(QK[:, h, :], QK[:, h, :], gqk[:, h], rt[:, s % 2:s % 2 + 1, :],
                                             ALU.mult, ALU.mult).then_inc(nm_done, 1)

                ch.loop(g, 20)
                for s in range(4):
                    ahead(G0["qk"] + g, s)
                    take8(m8s[:], Ws[:])
                    take8(m8p[:, s % 2, :], Wp[:, s % 2, 0:keys_of(s % 2)])
                    if s:
                        norm(s - 1)
                norm(3)

            loop(dve, GN["qk"], qk)
            ch.end(GN["qk"])

            dve.sem_inc(vk_done, 2)
            dve.wait_ge(o_ik, 48)

            def v(g):
                def copy(s):
                    c = bass.ds(g * 4 * P + P * s, P)
                    dve.wait_ge(vtr, g * 4 + (s + 1))
                    dve.tensor_copy(vtok[:, :, c], MB[s % 2][:, 0:2 * P].rearrange("p (i d) -> p i d", i=2))
                    dve.tensor_copy(v2[:, c], MB[s % 2][0:N_META, 2 * P:3 * P])
                    dve.tensor_copy(vs[:, c], MB[s % 2][0:NS, 3 * P:4 * P]).then_inc(vk_done, 1)

                ch.loop(g, 8)
                for s in range(4):
                    ahead(G0["v"] + g, s)
                    take8(m8s[:], Ws[:])
                    if s:
                        copy(s - 1)
                copy(3)

            loop(dve, GN["v"], v)
            ch.end(GN["v"])

            for qt in range(2):
                nk = keys_of(qt)
                ch.link(dve.tensor_tensor(Wp[:, qt, 0:nk], Wp[:, qt, 0:nk], Sp[:, qt, 0:nk], ALU.is_equal))
                ch.link(dve.tensor_scalar(Wp[:, qt, 0:nk], Wp[:, qt, 0:nk], NEG, None, ALU.mult))
            sbank = [SB[0], SB[1], TB[0], TB[1]]

            def p_logits(i):
                qt, h = i // H, i % H
                nk, z0 = keys_of(qt), P * (1 - qt)
                row = Lp[:, i % 2, 0:nk]
                dve.wait_ge(p_qk, i + 1)
                if i == 0:
                    dve.wait_ge(tb_ld, 16)
                if i >= 2:
                    dve.wait_ge(p_tr, i - 1)
                ins = dve.scalar_tensor_tensor(row, sbank[i % 4][:, 0:nk], SC, Tb[:, h, z0:z0 + nk], ALU.mult, ALU.add)
                ins.then_inc(p_lg, 1)
                dve.wait_ge(p_lg, i + 1)
                ch.link(dve.tensor_tensor(row, row, Wp[:, qt, 0:nk], ALU.add))
                dve.tensor_reduce(stat[:, 16 + i % 2:17 + i % 2], row, AX, ALU.max, negate=True).then_inc(p_max, 1)

            def p_norm(i):
                nk = keys_of(i // H)
                r = stat[:, 20 + i % 2:21 + i % 2]
                dve.wait_ge(p_exp, i + 1)
                ch.link(dve.reciprocal(r, r))
                dve.tensor_scalar(Lp[:, i % 2, 0:nk], Lp[:, i % 2, 0:nk], r, None, ALU.mult).then_inc(p_nrm, 1)

            def p_out(i):
                qt, h = i // H, i % H
                dve.wait_ge(p_pv, i + 1)
                dve.tensor_copy(oT[:, h, qt * P:qt * P + P], G[i % 2][:, 0:P]).then_inc(p_o, 1)

            p_logits(0)
            for i in range(2 * H):
                if i + 1 < 2 * H:
                    p_logits(i + 1)
                p_norm(i)
                if i:
                    p_out(i - 1)
            p_out(2 * H - 1)
            dve.wait_ge(ln_mm, H)
            for h in range(H):
                dve.scalar_tensor_tensor(LN[:, :, h, :], SB[0][0:NS, NS * h:NS * h + NS].rearrange("p (b q) -> p b q", b=B), SC,
                                         biasN[:, h:h + 1, :].to_broadcast([NS, B, Q]), ALU.mult, ALU.add).then_inc(ln_dn, 1)

            dve.sem_inc(kc_D, 1)
            dve.sem_inc(lg_done, 2)
            dve.wait_ge(ub_z, 1)

            def cz(g):
                ch.loop(g, 4)
                for s in range(4):
                    G_, b = G0["cz"] + g, g * 2 + s // 2
                    c = bass.ds(b, 1)
                    for j in range(4):
                        dve.wait_ge(k_tr, g * 16 + (4 * s + j + 5))
                        dve.tensor_copy(kTs[:, 4:8, :], TB[1][:].rearrange("p (h n) -> p h n", h=4)).then_inc(kc_D, 1)
                        ahead_quarter(G_, s, j)
                        if s % 2 == 0 and j == 0:
                            best8(m8s[:], Ws[:])
                        if s % 2 == 0 and j == 2:
                            taken8(m8s[:], Ws[:])
                    if s % 2 == 0:
                        continue
                    ev_wait(G_, s - 1)
                    done(G_, s)
                    dve.tensor_tensor(ub[:, c, UPAD:UP], G[1][:, None, 0:NP], sgt[:, None, 0:NP], ALU.mult)
                    dve.tensor_tensor(ub[:, c, UP:UW].rearrange("p o (b w) -> p (o b) w", b=B)[:, :, CTX:CTX + Q],
                                      G[1][:, NP:NT].rearrange("p (b q) -> p b q", b=B), sgt[:, NP:NT].rearrange("p (b q) -> p b q", b=B),
                                      ALU.mult).then_inc(ev[1], 1)
                    dve.wait_ge(kq_done, b + 1)
                    dve.scalar_tensor_tensor(L[:, :, c, :].rearrange("p t o x -> p t (o x)"), SB[s // 2][:].rearrange("p (t x) -> p t x", t=NPG), SC,
                                             biasS[:].rearrange("p t h q -> p t (h q)"), ALU.mult, ALU.add).then_inc(lg_done, 1)

            loop(dve, GN["cz"], cz)
            ch.end(GN["cz"])

            ch.wait()
            dve.wait_ge(lg_done, B + 2)
            dve.wait_ge(ln_dn, H)
            dve.tensor_tensor(Ws[:], Ws[:], Ss[:], ALU.is_equal).then_inc(x_e, 1)
            dve.wait_ge(x_tr, 1)
            ch.step(dve.tensor_scalar(MS[:], TB[0][:].rearrange("p (t x) -> p t x", t=NPG), NEG, None, ALU.mult))
            dve.tensor_scalar(e8[:], TB[1][0:Q, 0:NS], NEG, None, ALU.mult).then_inc(x_m, 1)
            ch.wait()
            for t in range(NPG):
                row = L[:, t].rearrange("p b (h q) -> p b h q", h=H)
                ch.step(dve.tensor_tensor(row, row, MS[:, t, :].rearrange("p (b o q) -> p b o q", b=B, o=1).to_broadcast([P, B, H, Q]), ALU.add))
            dve.wait_ge(x_rep, 1)
            dve.wait_ge(cb_ld, 32)
            ch.link(dve.tensor_tensor(MN[:], MB[0][0:NS, 0:NS], cblk[:], ALU.add))
            dve.tensor_tensor(LN[:], LN[:], MN[:].rearrange("p (b o q) -> p b o q", b=B, o=1).to_broadcast([NS, B, H, Q]), ALU.add).then_inc(x_mn, 1)
            dve.tensor_reduce(mx[:].rearrange("p i x -> p (i x)"), L[:].rearrange("p t b x -> p (b x) t"), AX, ALU.max).then_inc(x_mx, 1)
            dve.wait_ge(x_mt, 1)
            ch.step(dve.tensor_reduce(stat[:, 24:28], SB[0][:].rearrange("p (i x) -> p i x", i=4), AX, ALU.max))
            ch.link(dve.tensor_reduce(stat[:, 28:32], SB[1][:, 0:4 * NS].rearrange("p (i x) -> p i x", i=4), AX, ALU.max))
            ch.link(dve.tensor_tensor(stat[:, 32:36], stat[:, 24:28], stat[:, 28:32], ALU.max))
            for i in range(4):
                ins = dve.tensor_scalar(dg[:, i, :], ident[:], stat[:, 32 + i:33 + i], None, ALU.mult)
            ins.then_inc(x_dg, 1)
            dve.wait_ge(x_bc, 1)
            for t in range(NPG):
                row = L[:, t].rearrange("p b x -> p (b x)")
                dve.tensor_tensor(row, row, MB[1][:], ALU.subtract).then_inc(x_sub, 1)
            row = LN[:].rearrange("p b h q -> p (b h q)")
            dve.wait_ge(x_mn, 1)
            dve.tensor_tensor(row, row, MB[1][0:NS, :], ALU.subtract).then_inc(x_sub, 1)
            dve.wait_ge(x_exp, NPG)
            dve.tensor_reduce(mx[:].rearrange("p i x -> p (i x)"), L[:].rearrange("p t b x -> p (b x) t"), AX, ALU.add).then_inc(x_sm, 1)
            dve.wait_ge(x_den, 1)
            dve.reciprocal(rS[:].rearrange("p b h q -> p (b h q)"), G[0][:]).then_inc(x_rs, 1)

            taps = (CW + 1) // 2

            def ga(g):
                ch.loop(g, 4 * CW)
                for s in range(4):
                    c = g * 2 + s // 2
                    one = ub[:, bass.ds(c, 1), :]
                    first = 0 if s % 2 == 0 else taps
                    for w in range(first, taps if s % 2 == 0 else CW):
                        if (w - first) % (taps // 4) == 0:
                            ahead_quarter(G0["ga"] + g, s, (w - first) // (taps // 4))
                        z = ya[:, s // 2, w % 2, :]
                        zs = z[:, SEQ:NQ].rearrange("p (b q) -> p b q", b=B)
                        xp = one[:, :, w:w + SEQ].rearrange("p o n -> p (o n)")
                        xq = one[:, :, UP:UW].rearrange("p o (b w) -> p (o b) w", b=B)[:, :, w:w + Q]
                        tap = wdw[:].rearrange("p c w -> p (c w)")[:, bass.ds(c * CW + w, 1)]
                        if w == 0:
                            bias = prm[:, bass.ds(c + R_BDW, 1)]
                            dve.wait_ge(yc_done, c + 1)
                            ch.step(dve.tensor_scalar(z[:, 0:SEQ], xp, tap, bias, ALU.mult, ALU.add))
                            ch.step(dve.tensor_scalar(zs, xq, tap, bias, ALU.mult, ALU.add))
                        elif w == 1:
                            ch.step(dve.tensor_scalar(z[:, 0:SEQ], xp, tap, None, ALU.mult))
                            ch.step(dve.tensor_scalar(zs, xq, tap, None, ALU.mult))
                        else:
                            ch.wait_back(3)
                            ch.step(dve.scalar_tensor_tensor(z[:, 0:SEQ], xp, tap, z[:, 0:SEQ], ALU.mult, ALU.add))
                            ch.wait_back(3)
                            ch.step(dve.scalar_tensor_tensor(zs, xq, tap, zs, ALU.mult, ALU.add))
                    if s % 2:
                        ch.wait()
                        z = ya[:, s // 2]
                        dve.tensor_tensor(z[:, 0, :], z[:, 0, :], z[:, 1, :], ALU.add).then_inc(cv_done, 1)

            loop(dve, GN["ga"], ga)

            dve.wait_ge(np_mm, 1)
            dve.wait_ge(os_done, B + 2)
            o = oT[:, :, SEQ:NQ]
            ch.end(GN["ga"])
            ch.link(dve.tensor_tensor(o, o, TB[0][:].rearrange("p (h x) -> p h x", h=H), ALU.add))
            o = o.rearrange("p h (b q) -> p h b q", b=B)
            dve.tensor_tensor(o, o, rS[:].rearrange("p b h q -> p h b q"), ALU.mult).then_inc(o_sc, 1)
            dve.wait_ge(oh_dn, 1)
            dve.tensor_tensor(OL[:], oT[:], OH[:].bitcast(F32), ALU.subtract).then_inc(ol_dn, 1)
            dve.wait_ge(mu_mm, 1)
            for c in range(CT):
                dve.scalar_tensor_tensor(ub[:, c, 0:NQ], MB[0][:, 0:NQ], -1.0 / CC, ub[:, c, 0:NQ], ALU.mult, ALU.add).then_inc(mu_dn, 1)
            dve.wait_ge(cs_rt, 1)
            ch.link(dve.reciprocal(crt[:], crt[:]))
            dve.wait_ge(mu_dn, CT)
            for c in range(CT):
                dve.tensor_tensor(ub[:, c, 0:NQ], ub[:, c, 0:NQ], crt[:], ALU.mult).then_inc(cy_dn, 1)
            for c in range(CT):
                dve.wait_ge(ch_dn, c + 1)
                dve.tensor_tensor(CL[:, c, :], ub[:, c, 0:NQ], CH[:, c, :].bitcast(F32), ALU.subtract).then_inc(cl_dn, 1)

            def merge(g):
                ch.loop(g, 2)
                for s in range(4):
                    ahead(G0["merge"] + g, s)
                    if s % 2 == 0:
                        continue
                    G_, f, z = G0["merge"] + g, g * 2 + s // 2, mt[:, s // 2:s // 2 + 1, :]
                    done(G_, s)
                    ch.step(dve.tensor_tensor(z, G[1][:, None, 0:NQ], SGA[:, bass.ds(f, 1), :], ALU.mult))
                    ev_wait(G_, s - 1)
                    dve.tensor_tensor(mu_[:], MB[s // 2][:, 0:NQ], gbs[:, s // 2, :], ALU.mult).then_inc(ev[1], 1)
                    dve.wait_ge(ev[1], 2 * G_ + (s // 2 + 2))
                    ch.wait()
                    dve.tensor_tensor(z, z, mu_[:, None, :], ALU.add).then_inc(m_dn, 1)
                    dve.wait_ge(mh_dn, f + 1)
                    dve.tensor_tensor(ML[:, bass.ds(f, 1), :], z, MH[:, bass.ds(f, 1), :].bitcast(F32), ALU.subtract).then_inc(ml_dn, 1)

            loop(dve, GN["merge"], merge)
            ch.end(GN["merge"])


            def out(g):
                for s in range(4):
                    G_, f = G0["out"] + g, bass.ds(g * 4 + s, 1)
                    ahead(G_, s)
                    done(G_, s)
                    dve.tensor_tensor(hT[:, f, :], G[s % 2][:, None, 0:NQ], hT[:, f, :], ALU.add).then_inc(ev[s % 2], 1)
                    dve.wait_ge(xh_dn, g * 4 + (s + 1))
                    dve.scalar_tensor_tensor(XL[:, f, 0:NQ], hT[:, f, :], prm[:, bass.ds(g * 4 + (s + R_GFFN), 1)],
                                             XH[:, f, 0:NQ].bitcast(F32), ALU.mult, ALU.subtract).then_inc(xl_dn, 1)

            dve.wait_ge(h_ld[0], 16)
            out(0)
            dve.wait_ge(h_ld[1], 16)
            with dve.Fori(1, GN["out"]) as g:
                out(g)
            dve.wait_ge(rf_sq, 1)
            dve.reciprocal(rf[:], rf[:]).then_inc(rf_dn, 1)
            dve.wait_ge(rf_dn, 1)

            for n, (k0, m) in enumerate(PARTS):
                def gu(g):
                    for s in range(4):
                        G_, f = G0[f"gu{n}"] + g, g * 2 + s // 2
                        ahead(G_, s)
                        done(G_, s)
                        if s % 2 == 0:
                            dve.tensor_tensor(gt[:, s // 2, :], G[0][:, 0:NQ], rf[:], ALU.mult).then_inc(ev[0], 1)
                            continue
                        dve.tensor_tensor(ut[:], G[1][:, 0:NQ], rf[:], ALU.mult).then_inc(ev[1], 1)
                        dve.wait_ge(ev[1], 2 * G_ + (s // 2 + 2))
                        dve.wait_ge(si_dn, f + (k0 + 1))
                        dve.tensor_tensor(at2[:, s // 2, :], gt[:, s // 2, :], ut[:], ALU.mult).then_inc(ac_dn, 1)
                        dve.wait_ge(ah_dn, f + (k0 + 1))
                        dve.tensor_tensor(ML[:, bass.ds(f, 1), :], at2[:, s // 2:s // 2 + 1, :], MH[:, bass.ds(f, 1), :].bitcast(F32),
                                          ALU.subtract).then_inc(al_dn, 1)

                loop(dve, GN[f"gu{n}"], gu)
                final = n == len(PARTS) - 1

                def dn(g, last=False):
                    for s in range(4):
                        G_, f = G0[f"dn{n}"] + g, bass.ds(g * 4 + s, 1)
                        ahead(G_, s, last)
                        done(G_, s)
                        to = at2[:, s % 2:s % 2 + 1, :] if final else hT[:, f, :]
                        dve.tensor_tensor(to, G[s % 2][:, None, 0:NQ], hT[:, f, :], ALU.add).then_inc(ev[s % 2], 1)

                if final:
                    loop(dve, GN[f"dn{n}"] - 1, dn)
                    dn(GN[f"dn{n}"] - 1, True)
                else:
                    loop(dve, GN[f"dn{n}"], dn)

        @block.tensor
        def _(pe):
            def tr(out, src):
                n = src.shape[0]
                return pe.transpose(out, src, ident[0:n, 0:n])

            def mm(out, lhsT, rhs, start=True, stop=True):
                return pe.matmul(out, lhsT, rhs, start=start, stop=stop, skip_group_check=True)

            def split_mm(out, s, k, hi, lo, start, stop):
                pe.matmul(out, WH[:, s % 2, k], hi, start=start, stop=False)
                pe.matmul(out, WH[:, s % 2, k], lo, start=False, stop=False)
                return pe.matmul(out, WL[:, s % 2, k], hi, start=False, stop=stop)

            def ready(G_, s):
                pe.wait_ge(ev[s % 2], 2 * G_ + (s // 2 + 1))

            def products(G_, s, tiles, kt, product):
                for k in tiles:
                    if k % 4 == 0:
                        whole = k + 4 >= kt
                        pe.wait_ge(lo_done, 16 * G_ + (4 * s + (4 if whole else k // 4 + 1)))
                    ins = product(k)
                    if k == kt - 1:
                        ins.then_inc(mm_done, 4 - k // 4)
                    elif k % 4 == 3:
                        ins.then_inc(mm_done, 1)

            def unit(G_, s, n, hi, lo, kt=KT, ready_sem=None, ready_from=0):
                ready(G_, s)

                def product(k):
                    if ready_sem is not None and s == 0 and k % 4 == 0:
                        pe.wait_ge(ready_sem, ready_from + min(k + 4, kt))
                    return split_mm(G[s % 2][:, 0:n], s, k, hi(k), lo(k), k == 0, k == kt - 1)

                products(G_, s, range(kt), kt, product)

            def x_all(G_, s):
                unit(G_, s, NT, lambda k: XH[:, k, :], lambda k: XL[:, k, :])

            def x_out(G_, s):
                unit(G_, s, NQ, lambda k: XH[:, k, T0C:NT], lambda k: XL[:, k, T0C:NT])

            def lagged(G_, main, side):
                for s in range(4):
                    main(G_, s)
                    if s:
                        side(s - 1)
                side(3)

            pe.wait_ge(pool_init, 2)
            pe.wait_ge(c_ld, 176)
            tr(TB[0][:, 0:R_N], prow[:])
            for c in range(CT):
                ins = tr(TB[1][:, CW * c:CW * c + CW], wrow[:, P * c:P * c + P])
            ins.then_inc(a_par, 1)
            mm(SB[0][0:H, 0:RELW], relx[:], oh[:, OH_G:OH_G + RELW])
            for q in range(Q):
                mm(SB[1][:, H * q:H * q + H], oh[:, OH_T7 + P * q:OH_T7 + P * q + P], relx[:])
                mm(MB[0][0:NS, H * q:H * q + H], oh[:, OH_NEW + NS * q:OH_NEW + NS * q + NS], relx[:])
            mm(SB[1][:, Q * H:Q * H + H], oh[:, OH_FAR:OH_FAR + P], relx[:]).then_inc(a_tab, 1)
            pe.wait_ge(a_prm, 1)
            pe.wait_ge(a_bias, 1)
            pe.wait_ge(a_xs, 3)
            banks = [TB[0], TB[1], SB[0], SB[1]]
            for k in range(2 * KT):
                if 4 <= k < KT + 4:
                    pe.wait_ge(a_lo, k - 3)
                elif k >= KT + 4:
                    pe.wait_ge(a_rawD if k % 2 else a_rawA, (k - KT - 4) // 2 + 1)
                src, f = (xs, k) if k < KT else (xtok, k - KT)
                for i, (t, n) in enumerate(XTILES):
                    ins = tr(banks[k % 4][:, t:t + n], src[0:n, i, P * f:P * f + P])
                ins.then_inc(a_tr, 1)

            def iq(g):
                for s in range(4):
                    x_out(G0["iq"] + g, s)

            loop(pe, GN["iq"], iq)
            for s in range(4):
                ready(G0["ikiw"], s)

                def product(k):
                    x = 8 * (s % 2) + k
                    return split_mm(MB[s // 2][:, 0:NT], s, k, XH[:, x, :], XL[:, x, :], x == 0, x == KT - 1)

                products(G0["ikiw"], s, range(8), 8, product)

            for s in range(2):
                pe.wait_ge(ev[s], 2 * (G0["ikiw"] + 1) + 1)
            pe.wait_ge(a_rawA, KT // 2)
            pe.wait_ge(a_rawD, KT // 2)
            for qt in range(2):
                tr(TB[0][:, IH * qt:IH * qt + IH], iwT[:, T0C + P * qt:T0C + P * qt + P])
            mm(TB[0][:, 2 * IH:2 * IH + NS], esel[:], iwT[:, NP:NT])
            for i, (t, n) in enumerate(XTILES):
                ins = tr(TB[1][0:n, ID * i:ID * i + ID], ikT[0:ID, t:t + n])
            ins.then_inc(d_setup, 1)
            sums = [G[0][0:NS, :], G[1][0:NS, :], MB[1][0:NS, 0:Q]]

            def zero(out, start):
                n = out.shape[1]
                return mm(out, zer[:, 0:out.shape[0]], biasS[:].rearrange("p t h q -> p (t h q)")[:, 0:n], start, not start)

            for out in sums:
                zero(out, True)

            def keys(b, j):
                pe.wait_ge(d_stage, b + 1)
                pe.wait_ge(d_cpA, b + 1)
                pe.wait_ge(d_cpD, b + 1)
                for t in range(NPG):
                    ins = tr(TB[t // 4][:, P * (t % 4):P * (t % 4) + P], ikb[:, j, t, :, :].rearrange("p r d -> p (r d)"))
                ins.then_inc(ik_tr, 1)

            def scores(b, j):
                pe.wait_ge(d_cpA, b + 2)
                pe.wait_ge(d_cpD, b + 2)
                pe.wait_ge(d_rlA, b + 1)
                pe.wait_ge(d_rlD, b + 1)
                mm(SB[0][:], iqb[:, j, :], ikTp[:, j, 0:512])
                mm(SB[1][:], iqb[:, j, :], ikTp[:, j, 512:PAST])
                mm(MB[0][:, 0:Q], iqb[:, j, :], ikT[:, bass.ds(b * Q + NP, Q)]).then_inc(idx_mm, 1)

            def total(b, j):
                pe.wait_ge(d_rlA, b + 2)
                pe.wait_ge(d_rlD, b + 2)
                mm(sums[0], iwb[:, j, :], rl[:, j, 0:512], False, False)
                mm(sums[1], iwb[:, j, :], rl[:, j, 512:PAST], False, False)
                mm(sums[2], iwb[:, j, :], rl[:, j, PAST:LS], False, False).then_inc(sum_mm, 1)

            def idx(g):
                b = g * 2
                keys(b, 0)
                scores(b, 0)
                keys(b + 1, 1)
                total(b, 0)
                scores(b + 1, 1)
                total(b + 1, 1)

            loop(pe, B // 2, idx)
            for out in sums:
                ins = zero(out, False)
            ins.then_inc(sum_mm, 1)
            for i in range(2 * IH):
                h, qt = i // 2, i % 2
                nk = keys_of(qt)
                rows = slice(ID * (h % 2), ID * (h % 2) + ID)
                if i >= 2:
                    pe.wait_ge(pp_relu, i - 1)
                mm(SB[i % 2][:, 0:nk], iqT[rows, h // 2, P * qt:P * qt + P], ikT[rows, 0:nk]).then_inc(pp_mm, 1)

            pe.wait_ge(d_ss, 1)

            def qk(g):
                def squares(s):
                    pe.wait_ge(sq_done, g * 4 + (s + 1))
                    pe.wait_ge(sqrt_done, g * 4 + (s + 1))
                    mm(MB[s % 2][:, 0:NT], ones[:], sq[:, s % 2, :]).then_inc(st_done, 1)

                lagged(G0["qk"] + g, x_all, squares)

            loop(pe, GN["qk"], qk)
            pe.wait_ge(sqrt_done, 2 + 2 * H)

            def v(g):
                def by_token(s):
                    G_ = G0["v"] + g
                    pe.wait_ge(ev[s % 2], 2 * G_ + (s // 2 + 2))
                    pe.wait_ge(vk_done, g * 4 + (s + 1))
                    for i, (t, n) in enumerate([(0, P), (P, P), (2 * P, N_META), (NP, NS)]):
                        ins = tr(MB[s % 2][0:n, P * i:P * i + P], vT[:, s % 2, t:t + n])
                    ins.then_inc(vtr, 1)

                lagged(G0["v"] + g, x_all, by_token)

            loop(pe, GN["v"], v)

            pe.wait_ge(vk_done, 2 + H)
            pe.wait_ge(nm_done, 2 + 2 * H)
            pe.wait_ge(pp_relu, 2 * IH)
            for s in range(2):
                pe.wait_ge(ev[s], 2 * G0["cz"] + 1)
            sbank = [SB[0], SB[1], TB[0], TB[1]]

            def p_logits(i):
                qt, h = i // H, i % H
                if i >= 4:
                    pe.wait_ge(p_lg, i - 3)
                mm(sbank[i % 4][:, 0:keys_of(qt)], QK[:, h, T0C + P * qt:T0C + P * qt + P], QK[:, H + h, 0:keys_of(qt)]).then_inc(p_qk, 1)

            def p_turn(i):
                full = i // H + 1
                pe.wait_ge(p_nrm, i + 1)
                if i >= 2:
                    pe.wait_ge(p_cp, i - 1)
                for k in range(full):
                    tr(MB[i % 2][:, P * k:P * k + P], Lp[:, i % 2, P * k:P * k + P])
                tr(MB[i % 2][0:N_META, P * full:P * full + P], Lp[:, i % 2, P * full:P * full + N_META]).then_inc(p_tr, 1)

            def p_values(i):
                full, h = i // H + 1, i % H
                c = slice(P * h, P * h + P)
                pe.wait_ge(p_cp, i + 1)
                if i >= 2:
                    pe.wait_ge(p_o, i - 1)
                for k in range(full):
                    mm(G[i % 2][:, 0:P], vtok[:, k, c], pT[:, i % 2, k, :], k == 0, False)
                last = vtok[0:N_META, 1, c] if full == 1 else v2[:, c]
                mm(G[i % 2][:, 0:P], last, pT[0:N_META, i % 2, full, :], False, True).then_inc(p_pv, 1)

            for i in range(2):
                p_logits(i)
            for i in range(2 * H):
                if i + 2 < 2 * H:
                    p_logits(i + 2)
                p_turn(i)
                if i:
                    p_values(i - 1)
            p_values(2 * H - 1)
            pe.wait_ge(p_lg, 2 * H)
            for h in range(H):
                if h >= 2:
                    pe.wait_ge(ko_cp, h - 1)
                for i, (t, n) in enumerate(XTILES):
                    ins = tr(TB[h % 2][0:n, P * i:P * i + P], QK[:, H + h, t:t + n])
                ins.then_inc(ko_tr, 1)
                mm(SB[0][0:NS, NS * h:NS * h + NS], QK[:, H + h, NP:NT], QK[:, h, NP:NT]).then_inc(ln_mm, 1)
            pe.wait_ge(sc_ld, 32)
            pe.wait_ge(p_cp, 2 * H)
            for c in range(CT):
                if c >= 2:
                    pe.wait_ge(sc_cp, c - 1)
                for i in range(2):
                    ins = tr(MB[c % 2][:, 4 * CTX * i:4 * CTX * i + 4 * CTX], sct[:, i, P * c:P * c + P])
                ins.then_inc(sc_tr, 1)

            pe.wait_ge(p_o, 2 * H)
            pe.wait_ge(ko_cp, H)
            pe.wait_ge(ln_dn, H)
            pe.wait_ge(qs_dn, 1)

            def cz(g):
                for s in range(4):
                    G_, b = G0["cz"] + g, g * 2 + s // 2
                    for j in range(4):
                        n, t = g * 16 + (4 * s + j), 4 * (s % 2) + j
                        pe.wait_ge(k_ld[j], g * 64 + 16 * (s + 1))
                        pe.wait_ge(kc_A, n + 1)
                        pe.wait_ge(kc_D, n + 1)
                        for h in range(H):
                            ins = tr(TB[h // 4][:, P * (h % 4):P * (h % 4) + P], kst[:, j, P * h:P * h + P])
                        ins.then_inc(k_tr, 1)
                        if j == 0:
                            ready(G_, s)
                        products(G_, s, range(4 * j, 4 * j + 4), KT,
                                 lambda k: split_mm(G[s % 2][:, 0:NT], s, k, XH[:, k, :], XL[:, k, :], k == 0, k == KT - 1))
                        pe.wait_ge(kc_A, n + 2)
                        pe.wait_ge(kc_D, n + 2)
                        if t == 0:
                            pe.wait_ge(lg_done, b + 1)
                        for h in range(H):
                            ins = mm(SB[s // 2][:, NS * t + Q * h:NS * t + Q * h + Q], kTs[:, h, :], qs[:, h, bass.ds(b * Q, Q)],
                                     t == 0 and h == 0, t == NPG - 1 and h == H - 1)
                    if s % 2:
                        ins.then_inc(kq_done, 1)

            loop(pe, GN["cz"], cz)

            for s in range(2):
                pe.wait_ge(ev[s], 2 * G0["ga"] + 1)
            pe.wait_ge(lg_done, B + 2)
            pe.wait_ge(u_s, 1)
            for i in range(4):
                for c in range(4):
                    ct = 4 * (i % 2) + c
                    src = ub[:, ct, UP - CTX:UP] if i < 2 else uss[:, ct].rearrange("p b q -> p (b q)")
                    out = TB[i][0:CTX, P * c:P * c + P] if i < 2 else SB[i - 2][0:NS, P * c:P * c + P]
                    ins = tr(out, src)
                ins.then_inc(u_tr, 1)
            pe.wait_ge(u_cp, 2)
            pe.wait_ge(x_e, 1)
            for t in range(NPG):
                tr(TB[0][:, NS * t:NS * t + NS], Ws[:, PAGE * t:PAGE * t + PAGE])
            tr(TB[1][0:Q, 0:NS], Ws[:, PAST:LS]).then_inc(x_tr, 1)
            pe.wait_ge(x_m, 1)
            pe.wait_ge(cb_ld, 32)
            mm(MB[0][0:NS, 0:NS], crp[:], e8[:]).then_inc(x_rep, 1)
            pe.wait_ge(x_mx, 1)
            pe.wait_ge(x_mn, 1)
            pe.wait_ge(u_cp, 4)
            for i in range(4):
                tr(SB[0][:, P * i:P * i + P], mx[:, i, :])
                ins = tr(SB[1][:, NS * i:NS * i + NS], LN[:].rearrange("p b h q -> p (b h q)")[:, P * i:P * i + P])
            ins.then_inc(x_mt, 1)
            pe.wait_ge(x_dg, 1)
            mm(MB[1][:], ones[:], dg[:].rearrange("p i x -> p (i x)")).then_inc(x_bc, 1)
            pe.wait_ge(x_sm, 1)
            pe.wait_ge(x_exp, NPG + 1)
            mm(G[0][:], ones[:], mx[:].rearrange("p i x -> p (i x)"), True, False)
            mm(G[0][:], ones[0:NS, :], LN[:].rearrange("p b h q -> p (b h q)"), False, True).then_inc(x_den, 1)
            pe.wait_ge(x_rs, 1)

            def ga(g):
                for s in range(4):
                    G_, b = G0["ga"] + g, g * 2 + s // 2
                    ready(G_, s)
                    for j in range(4):
                        n, t = g * 16 + (4 * s + j), 4 * (s % 2) + j
                        products(G_, s, range(4 * j, 4 * j + 4), KT,
                                 lambda k: split_mm(G[s % 2][:, 0:NQ], s, k, XH[:, k, T0C:NT], XL[:, k, T0C:NT], k == 0, k == KT - 1))
                        pe.wait_ge(v_ld[j], g * 64 + 16 * (s + 1))
                        if t == 0:
                            pe.wait_ge(os_done, b + 1)
                        for h in range(H):
                            ins = mm(SB[s // 2][:, Q * h:Q * h + Q], vst[:, j, P * h:P * h + P], L[:, t, bass.ds(b, 1), Q * h:Q * h + Q].rearrange("p o q -> p (o q)"),
                                     t == 0 and h == 0, t == NPG - 1 and h == H - 1)
                        ins.then_inc(v_used, 1)

            loop(pe, GN["ga"], ga)

            for h in range(H):
                ins = mm(TB[0][:, NS * h:NS * h + NS], vs[:, P * h:P * h + P], LN[:, :, h, :])
            ins.then_inc(np_mm, 1)
            pe.wait_ge(yc_done, CT + 2)
            for c in range(CT):
                ins = mm(MB[0][:, 0:NQ], ones[:], ub[:, c, 0:NQ], c == 0, c == CT - 1)
            ins.then_inc(mu_mm, 1)
            for c in range(CT):
                pe.wait_ge(cs_sq, c + 1)
                mm(MB[1][:, 0:NQ], ones[:], csq[:, c % 2, :], c == 0, c == CT - 1).then_inc(va_mm, 1)

            pe.wait_ge(ol_dn, 1)
            pe.wait_ge(cl_dn, CT)

            def merge(g):
                for s in range(4):
                    G_ = G0["merge"] + g
                    if s % 2 == 0:
                        x_out(G_, s)
                        continue
                    ready(G_, s)

                    def product(k):
                        hi, lo, out = (OH, OL, G[1]) if k < H else (CH, CL, MB[s // 2])
                        return split_mm(out[:, 0:NQ], s, k, hi[:, k % H, :], lo[:, k % H, :], k % H == 0, k % H == H - 1)

                    products(G_, s, range(KT), KT, product)

            loop(pe, GN["merge"], merge)

            pe.wait_ge(ev[1], 2 * G0["out"] + 1)
            total_sq = MB[0][:, 0:NQ]
            zero(total_sq, True)

            def split_hidden(G_, s, kt=KT, ready_sem=ml_dn, ready_from=0):
                unit(G_, s, NQ, lambda k: MH[:, k, :], lambda k: ML[:, k, :], kt, ready_sem, ready_from)

            def out(g):
                def squares(s):
                    pe.wait_ge(h_sq, g * 4 + (s + 1))
                    mm(total_sq, ones[:], sq2[:, s % 2, :], False, False).then_inc(h_st, 1)

                lagged(G0["out"] + g, split_hidden, squares)

            loop(pe, GN["out"], out)
            zero(total_sq, False).then_inc(h_st, 1)

            for n, (k0, m) in enumerate(PARTS):
                def gu(g):
                    for s in range(4):
                        unit(G0[f"gu{n}"] + g, s, NQ, lambda k: XH[:, k, 0:NQ], lambda k: XL[:, k, 0:NQ], KT, xl_dn)

                loop(pe, GN[f"gu{n}"], gu)

                def dn(g):
                    for s in range(4):
                        split_hidden(G0[f"dn{n}"] + g, s, m, al_dn, k0)

                def dn_out(g):
                    G_ = G0[f"dn{n}"] + g

                    def by_token(s):
                        pe.wait_ge(ev[s % 2], 2 * G_ + (s // 2 + 2))
                        pe.wait_ge(y_cp, g * 4 + (s + 1))
                        for i, (t, w) in enumerate(QTILES):
                            ins = tr(MB[s % 2][0:w, P * i:P * i + P], at2[:, s % 2, t:t + w])
                        ins.then_inc(y_tr, 1)

                    lagged(G_, lambda G_, s: split_hidden(G_, s, m, al_dn, k0), by_token)

                if n < len(PARTS) - 1:
                    loop(pe, GN[f"dn{n}"], dn)
                else:
                    pe.wait_ge(rf_sq, 1)
                    loop(pe, GN[f"dn{n}"], dn_out)


_INS = ["x_prompt", "x_sample", "cache_k", "cache_v", "cache_ik", "state_conv", "page_table", "meta_tokens", "rel_bias",
        "norm_mix_g", "w_in", "q_norm_g", "k_norm_g", "w_attn_br", "w_dw", "b_dw", "ln_conv_g", "ln_conv_b", "w_conv_br",
        "w_out", "norm_ffn_g", "w_ffn_gate", "w_ffn_up", "w_ffn_down"]
_OUTS = [("y_prompt", (1, SEQ, D)), ("y_sample", (B, Q, D)), ("k_prompt", (1, 1, NP, H, P)), ("v_prompt", (1, 1, NP, H, P)),
         ("ik_prompt", (1, 1, NP, ID)), ("conv_prompt", (1, 1, CTX, CC)), ("k_sample", (1, B, Q, H, P)),
         ("v_sample", (1, B, Q, H, P)), ("ik_sample", (1, B, Q, ID)), ("conv_sample", (1, B, CTX, CC))]


def _constants():
    import math
    import numpy as np

    def bucket(rel):
        n = np.maximum(rel, 0)
        exact = BUCKETS // 2
        nf = np.maximum(n, 1).astype(np.float32)
        large = exact + (np.log(nf / np.float32(exact)) / np.float32(math.log(MAX_DIST / exact)) * np.float32(BUCKETS - exact)).astype(np.int32)
        return np.where(n < exact, n, np.minimum(large, BUCKETS - 1))

    p, q, y = np.arange(P), np.arange(Q), np.arange(RELW)
    j = np.arange(NS) % Q
    rel = np.concatenate([NP - 1 - y, (P + q[:, None] - p[None, :]).ravel(), np.maximum(q[:, None] - j[None, :], 0).ravel(),
                          np.full(P, PAST)])
    assert rel.size == OH_N
    oh = np.zeros((BUCKETS + 1, OH_N), np.float32)
    oh[np.where(rel < 0, BUCKETS, bucket(rel)), np.arange(OH_N)] = 1
    row = np.arange(NS)
    seen = lambda ok: np.where(ok, np.float32(3.4e38), np.float32(OUT_OF_REACH)).astype(np.float32)
    qt, key = np.arange(2)[None, :, None], np.arange(NP)[None, None, :]
    return {
        "c_ident": np.eye(P, dtype=np.float32),
        "c_oh": oh,
        "c_esel": (np.arange(IH)[:, None] == p[None, :] // Q).astype(np.float32),
        "c_qm": (p[:, None] % Q == q[None, :]).astype(np.float32),
        "c_cms": seen(q[None, :] <= row[:, None] % Q),
        "c_cmp": seen(key <= N_META + P * qt + p[:, None, None]),
        "c_blk": np.where((row[:, None] // Q == row[None, :] // Q) & (row[:, None] % Q <= row[None, :] % Q), 0, NEG).astype(np.float32),
        "c_rep": (q[:, None] == row[None, :] % Q).astype(np.float32),
    }


def kernel(**inputs):
    import numpy as np
    import concourse.bacc as bacc
    from concourse.bass_utils import run_bass_kernel_spmd as run

    nc = bacc.Bacc("TRN2", target_bir_lowering=False, num_devices=1)
    arrays, ins, outs = {}, {}, {}
    given = {name: np.ascontiguousarray(inputs[name]) for name in _INS}
    for name, a in {**given, **_constants()}.items():
        arrays[f"in_{name}"] = a
        ins[name] = nc.dram_tensor(f"in_{name}", a.shape, mybir.dt.from_np(a.dtype), kind="ExternalInput").ap()
    for i, (name, shape) in enumerate(_OUTS):
        outs[name] = nc.dram_tensor(f"out_{i}", shape, F32, kind="ExternalOutput").ap()
    layer(nc, ins, outs)
    r = run(nc, [arrays], core_ids=[0])
    return tuple(r.results[0][f"out_{i}"] for i in range(len(_OUTS)))
```

```python
from contextlib import ExitStack

import concourse.bass as bass
from concourse import mybir

F32 = mybir.dt.float32
F32R = mybir.dt.float32r
I32 = mybir.dt.int32
ALU = mybir.AluOpType
ACT = mybir.ActivationFunctionType
AX = mybir.AxisListType.X

P = 128
D = 2048
KT = D // P
N_META, SEQ, B, Q = 16, 256, 8, 8
NS = B * Q
NP = N_META + SEQ
NT = NP + NS
NQ = SEQ + NS
T0C = N_META
H = 8
IH, ID = 16, 64
PAST, PAGE = 1024, 128
NPG = PAST // PAGE
LS = PAST + Q
TOPK_P, TOPK_S = SEQ // 4, 256
CC, CW = 1024, 31
CT = CC // P
CTX = CW - 1
FF = 5632
EPS = 1e-6
NEG = -1e30
OUT_OF_REACH = -3.0e38
TAKEN = -3.4e38
BUCKETS, MAX_DIST = 32, 128

C_Q, C_K, C_V = 0, 1024, 2048
C_IQ, C_IK, C_IW = 3072, 4096, 4160
C_CZ = 4176
C_GA = C_CZ + 2 * CC
C_GB = C_GA + D

UP = N_META - 2 + NP
UPAD = CTX - N_META
UW = UP + B * (CTX + Q)
RELW = 400

OH_G, OH_T7, OH_NEW, OH_FAR, OH_N = 0, RELW, RELW + Q * P, RELW + Q * P + Q * NS, RELW + Q * P + Q * NS + P

R_GMIX, R_GFFN, R_BDW, R_LNG, R_LNB, R_QG, R_KG, R_N = 0, 16, 32, 40, 48, 56, 57, 58


class Chain:

    def __init__(self, eng, sem):
        self.eng, self.sem, self.start, self.g, self.per, self.k = eng, sem, 0, 0, 0, 0

    def loop(self, g, per):
        self.g, self.per, self.k = g, per, 0

    def end(self, n):
        assert self.k == self.per, (self.k, self.per)
        self.start += n * self.per
        self.g = self.per = self.k = 0

    def value(self):
        return self.start + self.g * self.per + self.k if self.per else self.start

    def step(self, ins):
        ins.then_inc(self.sem, 1)
        if self.per:
            self.k += 1
        else:
            self.start += 1

    def wait(self):
        self.eng.wait_ge(self.sem, self.value())

    def rest(self):
        self.wait()
        self.eng.memset(self.spare, 0.0)

    def wait_back(self, n):
        self.eng.wait_ge(self.sem, self.value() - n)

    def link(self, ins):
        self.step(ins)
        self.wait()


def loop(eng, n, body):
    if n == 1:
        body(0)
    else:
        with eng.Fori(0, n) as g:
            body(g)



def place(persistent, transient):
    def size(shape):
        n = 4
        for x in shape[1:]:
            n *= x
        return (n + 31) // 32 * 32

    top, where = 16512, {}
    for name, shape, _ in persistent:
        where[name] = top
        top += size(shape)
    base, placed = top, []
    for name, shape, _, first, last in sorted(transient, key=lambda t: PLACING.index(t[0])):
        off = base
        for o, n, f, l in sorted(placed):
            if f <= last and first <= l and o < off + size(shape) and off < o + n:
                off = o + n
        assert off + size(shape) <= 229344, (name, off, size(shape))
        placed.append((off, size(shape), first, last))
        where[name] = off
    return where


(ST_A, ST_IQ, ST_IKIW, ST_INDEX, ST_QK, ST_V, ST_PROMPT, ST_KOUT, ST_CZ, ST_SOFTMAX, ST_GA, ST_OSPLIT, ST_NORM,
 ST_MERGE, ST_OUT, ST_FFN) = range(16)

PERSISTENT = [
    ("XH", [P, KT, NT], F32R), ("XL", [P, KT, NT], F32R),
    ("RAW", [P, 4, KT, P], F32), ("WH", [P, 2, KT, P], F32R), ("WL", [P, 2, KT, P], F32R),
    ("ident", [P, P], F32), ("ones", [P, P], F32), ("zer", [P, P], F32),
    ("prm", [P, R_N], F32), ("gqk", [P, 2 * H], F32), ("wdw", [P, CT, CW], F32),
    ("eps", [P, 1], F32), ("stat", [P, 64], F32), ("ptab", [1, B * NPG], I32),
    ("biasS", [P, NPG, H, Q], F32), ("biasN", [NS, H, Q], F32),
]
TRANSIENT = [
    ("hT", [P, KT, NQ], F32, ST_OUT, ST_FFN),
    ("SGA", [P, KT, NQ], F32, ST_GA, ST_FFN),
    ("ML", [P, KT, NQ], F32R, ST_MERGE, ST_FFN),
    ("OH", [P, H, NQ], F32R, ST_OSPLIT, ST_MERGE), ("OL", [P, H, NQ], F32R, ST_OSPLIT, ST_MERGE),
    ("ub", [P, CT, UW], F32, ST_KOUT, ST_NORM),
    ("oT", [P, H, NQ], F32, ST_PROMPT, ST_OSPLIT),
    ("vs", [NS, CC], F32, ST_V, ST_OSPLIT),
    ("LN", [NS, B, H, Q], F32, ST_KOUT, ST_OSPLIT), ("rS", [P, B, H, Q], F32, ST_SOFTMAX, ST_OSPLIT),
    ("Ss", [NS, LS], F32, ST_INDEX, ST_SOFTMAX), ("Ws", [NS, LS], F32, ST_INDEX, ST_SOFTMAX),
    ("m8s", [NS, 8], F32, ST_INDEX, ST_CZ),
    ("L", [P, NPG, B, H * Q], F32, ST_CZ, ST_GA), ("ya", [P, 2, 2, NQ], F32, ST_GA, ST_GA),
    ("Sp", [P, 2, NP], F32, ST_INDEX, ST_PROMPT), ("Wp", [P, 2, NP], F32, ST_INDEX, ST_PROMPT),
    ("m8p", [P, 2, 8], F32, ST_INDEX, ST_QK),
    ("CH", [P, CT, NQ], F32R, ST_NORM, ST_MERGE), ("CL", [P, CT, NQ], F32R, ST_NORM, ST_MERGE),
    ("xtok", [P, 3, D], F32, ST_A, ST_A), ("xs", [P, 3, D], F32, ST_A, ST_A),
    ("xTs", [P, KT, NQ], F32, ST_A, ST_A), 
    ("oh", [33, OH_N], F32, ST_A, ST_IKIW), ("wrow", [CW, CC], F32, ST_A, ST_A),
    ("prow", [R_N, P], F32, ST_A, ST_A), ("relx", [33, H], F32, ST_A, ST_IKIW),
    ("gsb", [H, RELW], F32, ST_A, ST_QK),
    ("esel", [IH, P], F32, ST_A, ST_INDEX), ("qm", [P, Q], F32, ST_A, ST_INDEX),
    ("cms", [NS, Q], F32, ST_A, ST_INDEX), ("cmp", [P, 2, NP], F32, ST_A, ST_INDEX),
    ("ikst", [P, B, NPG, ID], F32, ST_IQ, ST_INDEX),
    ("iqT", [P, H, SEQ], F32, ST_IQ, ST_INDEX), ("iqs", [P, B, H, 2, Q], F32, ST_IQ, ST_INDEX),
    ("ikT", [P, NT], F32, ST_IKIW, ST_INDEX), ("iwT", [IH, NT], F32, ST_IKIW, ST_INDEX),
    ("IW", [P, B, NS + Q], F32, ST_IKIW, ST_INDEX), ("iktok", [P, 3, ID], F32, ST_INDEX, ST_QK),
    ("iwtok", [P, 2, IH], F32, ST_INDEX, ST_INDEX),
    ("iqb", [P, 2, P], F32, ST_INDEX, ST_INDEX), ("iwb", [P, 2, NS], F32, ST_INDEX, ST_INDEX),
    ("ikb", [P, 2, NPG, 2, ID], F32, ST_INDEX, ST_INDEX), ("ikTp", [P, 2, PAST], F32, ST_INDEX, ST_INDEX),
    ("rl", [P, 2, LS], F32, ST_INDEX, ST_INDEX), ("rp", [P, 2, NP], F32, ST_INDEX, ST_INDEX),
    ("QK", [P, 2 * H, NT], F32, ST_QK, ST_KOUT),
    ("sq", [P, 2, NT], F32, ST_QK, ST_QK), ("rt", [P, 2, NT], F32, ST_QK, ST_QK),
    ("vT", [P, 2, NT], F32, ST_V, ST_V), ("vtok", [P, 2, CC], F32, ST_V, ST_KOUT),
    ("v2", [16, CC], F32, ST_V, ST_KOUT), ("Tb", [P, H, NP], F32, ST_V, ST_PROMPT),
    ("sct", [120, 2, CC], F32, ST_KOUT, ST_KOUT),
    ("Lp", [P, 4, NP], F32, ST_PROMPT, ST_PROMPT), ("pT", [P, 2, 3, P], F32, ST_PROMPT, ST_PROMPT),
    ("ktok", [P, 2, 3, 2 * P], F32, ST_KOUT, ST_KOUT), ("qs", [P, H, NS], F32, ST_KOUT, ST_CZ),
    ("kst", [P, 4, CC], F32, ST_CZ, ST_CZ), ("kTs", [P, H, P], F32, ST_CZ, ST_CZ),
    ("sgt", [P, NT], F32, ST_CZ, ST_CZ), ("cblk", [NS, NS], F32, ST_CZ, ST_SOFTMAX),
    ("crp", [Q, NS], F32, ST_CZ, ST_SOFTMAX), ("vst", [P, 4, CC], F32, ST_SOFTMAX, ST_GA),
    ("MS", [P, NPG, NS], F32, ST_SOFTMAX, ST_SOFTMAX), ("MN", [NS, NS], F32, ST_SOFTMAX, ST_SOFTMAX),
    ("e8", [Q, NS], F32, ST_SOFTMAX, ST_SOFTMAX), ("mx", [P, 4, P], F32, ST_SOFTMAX, ST_SOFTMAX),
    ("dg", [P, 4, P], F32, ST_SOFTMAX, ST_SOFTMAX), ("utok", [32, CC], F32, ST_SOFTMAX, ST_SOFTMAX), ("uss", [P, CT, B, Q], F32, ST_SOFTMAX, ST_SOFTMAX),
    ("ustok", [NS, CC], F32, ST_SOFTMAX, ST_SOFTMAX),
    ("csq", [P, 2, NQ], F32, ST_NORM, ST_NORM),
    ("crt", [P, NQ], F32, ST_NORM, ST_NORM),
    ("gbs", [P, 2, NQ], F32, ST_MERGE, ST_MERGE), ("mt", [P, 2, NQ], F32, ST_MERGE, ST_MERGE),
    ("mu_", [P, NQ], F32, ST_MERGE, ST_MERGE),
    ("sq2", [P, 2, NQ], F32, ST_OUT, ST_OUT), ("rf", [P, NQ], F32, ST_OUT, ST_FFN),
    ("gt", [P, 2, NQ], F32, ST_FFN, ST_FFN), ("ut", [P, NQ], F32, ST_FFN, ST_FFN),
    ("at", [P, 2, NQ], F32, ST_FFN, ST_FFN), ("ytok", [P, 4, 3, P], F32, ST_FFN, ST_FFN),
]
PLACING = ("iwtok vT oh Ws xtok SGA vst dg ustok ikT m8s m8p CH rS vs qs rl utok MS iqs QK cblk ub xTs rp esel ktok "
           "iqb ytok oT ikst LN e8 pT Ss ya wrow CL rf L MN gt prow rt kTs mt sq mu_ OL qm sgt Sp cms iqT crp sq2 IW "
           "ML ikTp xs cmp Wp v2 crt sct gsb at ut mx relx uss iktok Lp iwb gbs hT ikb Tb vtok OH csq kst iwT ").split()


def layer(nc, I, O):
    gscr = nc.dram_tensor("bias_scratch", (H, P, RELW), F32)
    xscr = nc.dram_tensor("xT_scratch", (D, NQ), F32).ap()

    def tiles(w):
        return w[0].rearrange("(k p) n -> p k n", p=P)

    w_in, w_a, w_c, w_o = tiles(I["w_in"]), tiles(I["w_attn_br"]), tiles(I["w_conv_br"]), tiles(I["w_out"])
    w_g, w_u, w_d = tiles(I["w_ffn_gate"]), tiles(I["w_ffn_up"]), tiles(I["w_ffn_down"])
    cache_k = I["cache_k"][0].rearrange("g s h d -> g s (h d)")
    cache_v = I["cache_v"][0].rearrange("g s h d -> g s (h d)")
    cache_ik = I["cache_ik"][0]
    POOL_PAGES = cache_ik.shape[0]

    PARTS = [(0, 16), (16, 16), (32, 12)]
    assert sum(m for _, m in PARTS) * P == FF
    plan = [("iq", 8), ("ikiw", 4), ("qk", 16), ("v", 8), ("cz", 16), ("ga", 16), ("merge", 32), ("out", 16)]
    for n, (_, m) in enumerate(PARTS):
        plan += [(f"gu{n}", 2 * m), (f"dn{n}", 16)]
    G0, GN, at = {}, {}, 0
    for name, n in plan:
        assert n % 4 == 0
        G0[name], GN[name] = at, n // 4
        at += n // 4
    GROUPS = at

    where = place(PERSISTENT, TRANSIENT)
    T = {}
    for name, shape, dt, *_ in PERSISTENT + TRANSIENT:
        T[name] = nc.alloc_sbuf_tensor_at(name, shape, dt, offset=where[name])
    T["MH"] = nc.alloc_sbuf_tensor_at("MH", [P, KT, NQ], F32R, offset=where["SGA"])

    XH, XL, RAW, WH, WL = T["XH"], T["XL"], T["RAW"], T["WH"], T["WL"]
    ident, ones, zer, prm, gqk, wdw, eps, stat = (T[x] for x in ("ident", "ones", "zer", "prm", "gqk", "wdw", "eps", "stat"))
    ptab, biasS, biasN = T["ptab"], T["biasS"], T["biasN"]
    hT, SGA, MH, ML, OH, OL, CH, CL = (T[x] for x in ("hT", "SGA", "MH", "ML", "OH", "OL", "CH", "CL"))
    ub, oT, vs, LN, rS, Ss, Ws, L, Sp, Wp = (T[x] for x in ("ub", "oT", "vs", "LN", "rS", "Ss", "Ws", "L", "Sp", "Wp"))
    m8s, m8p = T["m8s"], T["m8p"]
    xtok, xs, xTs, oh, wrow, prow, relx, gsb = (T[x] for x in ("xtok", "xs", "xTs", "oh", "wrow", "prow", "relx", "gsb"))
    esel, qm, cms, cmp_, ikst, iqT, iqs, ikT, iwT, IW = (T[x] for x in ("esel", "qm", "cms", "cmp", "ikst", "iqT", "iqs", "ikT", "iwT", "IW"))
    iktok, iwtok, iqb, iwb, ikb, ikTp, rl, rp = (T[x] for x in ("iktok", "iwtok", "iqb", "iwb", "ikb", "ikTp", "rl", "rp"))
    QK, sq, rt, vT, vtok, v2, Tb, sct, Lp, pT, ktok, qs = (T[x] for x in ("QK", "sq", "rt", "vT", "vtok", "v2", "Tb", "sct", "Lp", "pT", "ktok", "qs"))
    kst, kTs, sgt, cblk, crp, vst, MS, MN, e8, mx, dg = (T[x] for x in ("kst", "kTs", "sgt", "cblk", "crp", "vst", "MS", "MN", "e8", "mx", "dg"))
    uss = T["uss"]
    utok, ustok, ya, csq, crt, gbs, mt, mu_, sq2, rf, gt, ut, at2, ytok = (
        T[x] for x in ("utok", "ustok", "ya", "csq", "crt", "gbs", "mt", "mu_", "sq2", "rf", "gt", "ut", "at", "ytok"))

    XTILES = [(0, P), (P, P), (2 * P, NT - 2 * P)]
    QTILES = [(0, P), (P, P), (2 * P, NS)]

    def keys_of(qt):
        return N_META + P * (qt + 1)

    with ExitStack() as ctx:
        G, TB, SB, MB = ([ctx.enter_context(nc.psum_tensor(f"ps{n}{i}", [P, 512], F32)) for i in range(2)] for n in "GTSM")

        def sem(name):
            return ctx.enter_context(nc.semaphore(name))

        def sems(name, n):
            return [sem(f"{name}{i}") for i in range(n)]

        w_ld = sems("w_ld", 4)
        hi_done, lo_done, mm_done = sem("hi_done"), sem("lo_done"), sem("mm_done")
        ev = sems("ev", 2)
        id_ld, x_ld, c_ld, c2_ld, g_wr, x_wr, tb_ld = sem("id_ld"), sem("x_ld"), sem("c_ld"), sem("c2_ld"), sem("g_wr"), sem("x_wr"), sem("tb_ld")
        pool_init, pool_zero = sem("pool_init"), sem("pool_zero")
        a_par, a_prm, a_tab, a_bias, a_sqrt, a_rms, a_xs, a_tr = sem("a_par"), sem("a_prm"), sem("a_tab"), sem("a_bias"), sem("a_sqrt"), sem("a_rms"), sem("a_xs"), sem("a_tr")
        a_hi, a_lo, a_raw = sem("a_hi"), sem("a_lo"), sem("a_raw")
        act_ch, dve_ch = sem("act_ch"), sem("dve_ch")
        ik_ld, d_setup, d_iw, d_stage, d_page, ik_tr = sem("ik_ld"), sem("d_setup"), sem("d_iw"), sem("d_stage"), sem("d_page"), sem("ik_tr")
        d_cpA, d_cpD, idx_mm, d_rlA, d_rlD, sum_mm, d_ss = sem("d_cpA"), sem("d_cpD"), sem("idx_mm"), sem("d_rlA"), sem("d_rlD"), sem("sum_mm"), sem("d_ss")
        pp_mm, pp_relu, pp_acc, o_ik = sem("pp_mm"), sem("pp_relu"), sem("pp_acc"), sem("o_ik")
        sq_done, st_done, sqrt_done, nm_done, vtr, vk_done = sem("sq_done"), sem("st_done"), sem("sqrt_done"), sem("nm_done"), sem("vtr"), sem("vk_done")
        p_mask = sem("p_mask")
        p_qk, p_lg, p_max, p_exp, p_nrm, p_tr, p_cp, p_pv, p_o = (sem(x) for x in ("p_qk", "p_lg", "p_max", "p_exp", "p_nrm", "p_tr", "p_cp", "p_pv", "p_o"))
        ko_tr, ko_cp, ko_wr, v_wr, ln_mm, ln_dn, qs_dn = sem("ko_tr"), sem("ko_cp"), sems("ko_wr", 4), sem("v_wr"), sem("ln_mm"), sem("ln_dn"), sem("qs_dn")
        sc_ld, sc_tr, sc_cp, ub_z, cs_wr = sem("sc_ld"), sem("sc_tr"), sem("sc_cp"), sem("ub_z"), sem("cs_wr")
        k_ld, k_tr, kc_A, kc_D, kq_done, lg_done = sems("k_ld", 4), sem("k_tr"), sem("kc_A"), sem("kc_D"), sem("kq_done"), sem("lg_done")
        cb_ld, u_s, u_tr, u_cp, u_wr = sem("cb_ld"), sem("u_s"), sem("u_tr"), sem("u_cp"), sem("u_wr")
        x_e, x_tr, x_m, x_rep, x_mn, x_mx, x_mt, x_dg, x_bc, x_sub, x_exp, x_sm, x_den, x_rs = (
            sem(f"x_{n}") for n in ("e", "tr", "m", "rep", "mn", "mx", "mt", "dg", "bc", "sub", "exp", "sm", "den", "rs"))
        v_ld, v_used, os_done, cv_done, yc_done = sems("v_ld", 4), sem("v_used"), sem("os_done"), sem("cv_done"), sem("yc_done")
        np_mm, o_sc, oh_dn, ol_dn, mu_mm, mu_dn, cs_sq, va_mm, cs_rt, cy_dn, cs_si, ch_dn, cl_dn = (
            sem(x) for x in ("np_mm", "o_sc", "oh_dn", "ol_dn", "mu_mm", "mu_dn", "cs_sq", "va_mm", "cs_rt", "cy_dn", "cs_si", "ch_dn", "cl_dn"))
        m_dn, mh_dn, ml_dn = sem("m_dn"), sem("mh_dn"), sem("ml_dn")
        h_ld = sems("h_ld", 2)
        h_sq, h_st, xh_dn, xl_dn, rf_sq, rf_dn = (sem(x) for x in ( "h_sq", "h_st", "xh_dn", "xl_dn", "rf_sq", "rf_dn"))
        si_dn, ac_dn, ah_dn, al_dn, y_tr, y_cp = (sem(x) for x in ("si_dn", "ac_dn", "ah_dn", "al_dn", "y_tr", "y_cp"))
        y_wr = sems("y_wr", 4)

        block = ctx.enter_context(nc.Block())

        @block.sync
        def _(sp):
            sp.dma_start(ident[:], I["c_ident"]).then_inc(id_ld, 16)
            sp.dma_start(xtok[0:N_META, 0, :], I["meta_tokens"]).then_inc(x_ld, 16)
            xp = I["x_prompt"][0]
            sp.dma_start(xtok[N_META:P, 0, :], xp[0:P - N_META]).then_inc(x_ld, 16)
            sp.dma_start(xtok[:, 1, :], xp[P - N_META:2 * P - N_META]).then_inc(x_ld, 16)
            sp.dma_start(xtok[0:N_META, 2, :], xp[2 * P - N_META:SEQ]).then_inc(x_ld, 16)
            sp.dma_start(xtok[N_META:N_META + NS, 2, :], I["x_sample"].rearrange("b q d -> (b q) d")).then_inc(x_ld, 16)

            def load(G_, s, dst_a, src_a, dst_b, src_b, first=False):
                if not first:
                    sp.wait_ge(lo_done, 16 * G_ + (4 * s - 12))
                sp.dma_start(dst_a, src_a).then_inc(w_ld[s], 16)
                sp.dma_start(dst_b, src_b).then_inc(w_ld[s], 16)

            def columns(G_, s, w, col, k0=0, m=KT, first=False):
                c = bass.ds(col if isinstance(col, int) else sp.snap(col), P)
                load(G_, s, RAW[:, s, 0:8, :], w[:, k0:k0 + 8, c], RAW[:, s, 8:m, :], w[:, k0 + 8:k0 + m, c], first)

            for s in range(4):
                columns(0, s, w_in, C_IQ + P * s, first=True)
            for s in range(4):
                columns(1, s, w_in, C_IQ + P * (4 + s))
            for s in range(2):
                w = w_in[:, 8 * s:8 * s + 8, C_IK:C_IK + ID]
                load(G0["ikiw"], s, RAW[:, s, 0:8, 0:ID], w, RAW[:, s, 0:8, ID:P], w)
            for s in range(2):
                w = w_in[:, 8 * s:8 * s + 8, C_IW:C_IW + IH]
                load(G0["ikiw"], 2 + s, RAW[:, 2 + s, 0:4, 0:IH], w[:, 0:4], RAW[:, 2 + s, 4:8, 0:IH], w[:, 4:8])

            def stage(name, unit):
                def body(g):
                    for s in range(4):
                        unit(G0[name] + g, g, s)
                loop(sp, GN[name], body)

            stage("qk", lambda G_, g, s: columns(G_, s, w_in, g * 4 * P + (C_Q + P * s)))
            stage("v", lambda G_, g, s: columns(G_, s, w_in, g * 4 * P + (C_V + P * s)))
            stage("cz", lambda G_, g, s: columns(G_, s, w_in, g * 2 * P + (C_CZ + (CC if s % 2 == 0 else 0) + P * (s // 2))))
            stage("ga", lambda G_, g, s: columns(G_, s, w_in, g * 4 * P + (C_GA + P * s)))

            def merge_unit(G_, g, s):
                if s % 2 == 0:
                    columns(G_, s, w_in, g * 2 * P + (C_GB + P * (s // 2) - 2 * P))
                else:
                    c = bass.ds(g * 2 * P + (P * (s // 2) - 2 * P), P)
                    load(G_, s, RAW[:, s, 0:8, :], w_a[:, :, c], RAW[:, s, 8:16, :], w_c[:, :, c])

            with sp.Fori(1, GN["merge"] + 1) as g:
                for s in range(4):
                    merge_unit(g + (G0["merge"] - 1), g, s)
            stage("out", lambda G_, g, s: columns(G_, s, w_o, g * 4 * P + P * s))
            for n, (k0, m) in enumerate(PARTS):
                stage(f"gu{n}", lambda G_, g, s: columns(G_, s, w_u if s % 2 else w_g, g * 2 * P + P * (k0 + s // 2)))
                stage(f"dn{n}", lambda G_, g, s: columns(G_, s, w_d, g * 4 * P + P * s, k0, m))

        @block.gpsimd
        def _(pool):
            pool.memset(ones[:], 1.0)
            pool.memset(zer[:], 0.0)
            pool.memset(eps[:], EPS)
            pool.memset(stat[:], 1.0).then_inc(pool_init, 1)
            pool.wait_ge(pool_init, 1)
            pool.memset(relx[32:33, :], NEG).then_inc(pool_init, 1)
            pool.sem_inc(ev[0], 1)
            pool.sem_inc(ev[1], 1)
            small = [(oh[:], I["c_oh"]), (relx[0:BUCKETS, :], I["rel_bias"]),
                     (wrow[:], I["w_dw"][0])]
            for r, name, n in ((R_GMIX, "norm_mix_g", KT), (R_GFFN, "norm_ffn_g", KT), (R_BDW, "b_dw", CT), (R_LNG, "ln_conv_g", CT),
                               (R_LNB, "ln_conv_b", CT), (R_QG, "q_norm_g", 1), (R_KG, "k_norm_g", 1)):
                small.append((prow[r:r + n, :], I[name].rearrange("o (n p) -> (o n) p", p=P)))
            for dst, src in small:
                pool.dma_start(dst, src).then_inc(c_ld, 16)
            for dst, src in ((ptab[:], I["page_table"].rearrange("b (o n) -> o (b n)", o=1)), (esel[:], I["c_esel"]),
                             (qm[:], I["c_qm"]), (cms[:], I["c_cms"]), (cmp_[:], I["c_cmp"])):
                pool.dma_start(dst, src).then_inc(c2_ld, 16)
            pool.wait_ge(a_raw, KT)
            pool.dma_start(xscr.rearrange("(k p) n -> p k n", p=P), xTs[:]).then_inc(x_wr, 16)
            pool.wait_ge(x_wr, 16)
            pool.wait_ge(c2_ld, 80)
            pool.wait_ge(a_lo, KT)
            pool.memset(iqs[:], 0.0)
            pool.memset(IW[:], 0.0).then_inc(pool_zero, 1)

            def page(i):
                return pool.value_load(ptab[0:1, bass.ds(i, 1)], min_val=0, max_val=POOL_PAGES - 1)

            with pool.Fori(0, B) as b:
                for t in range(NPG):
                    pool.dma_start(ikst[:, bass.ds(b, 1), t, :], cache_ik[bass.ds(page(b * NPG + t), 1)].rearrange("o s d -> s o d")).then_inc(ik_ld, 16)
            pool.wait_ge(a_bias, 1)
            pool.dma_start(gscr.ap(), gsb[:, None, :].to_broadcast([H, P, RELW])).then_inc(g_wr, 16)
            pool.wait_ge(g_wr, 16)
            pool.wait_ge(d_iw, 1)
            pool.wait_ge(d_cpA, 1)
            pool.dma_start(O["ik_prompt"][0, 0, 0:2 * P].rearrange("(i p) d -> p i d", p=P), iktok[:, 0:2, :]).then_inc(o_ik, 16)
            pool.dma_start(O["ik_prompt"][0, 0, 2 * P:NP], iktok[0:NP - 2 * P, 2, :]).then_inc(o_ik, 16)
            pool.dma_start(O["ik_sample"][0].rearrange("b q d -> (b q) d"), iktok[NP - 2 * P:NT - 2 * P, 2, :]).then_inc(o_ik, 16)

            pool.sem_inc(sum_mm, 2)

            def staging(g):
                for j in range(2):
                    b = g * 2 + j
                    pool.wait_ge(sum_mm, b + 1)
                    pool.tensor_copy(iqb[:, j:j + 1, :], iqs[:, bass.ds(b, 1)].rearrange("p o h r q -> p o (h r q)"))
                    pool.tensor_copy(iwb[:, j, :], IW[:].rearrange("p b n -> p (b n)")[:, bass.ds(b * NS, NS)]).then_inc(d_stage, 1)

            loop(pool, B // 2, staging)

            pool.wait_ge(nm_done, 2 + 2 * H)
            pool.dma_start(Tb[:], bass.AP(tensor=gscr, offset=P - 1, ap=[[RELW - 1, P], [P * RELW, H], [1, NP]])).then_inc(tb_ld, 16)
            pool.dma_start(O["conv_sample"][0, :, 0:CTX - Q], I["state_conv"][0, :, Q:CTX]).then_inc(cs_wr, 16)
            pool.wait_ge(vk_done, 2 + H)
            vp = O["v_prompt"][0, 0].rearrange("t h d -> t (h d)")
            pool.dma_start(vp[0:2 * P].rearrange("(i p) n -> p i n", p=P), vtok[:]).then_inc(v_wr, 16)
            pool.dma_start(vp[2 * P:NP], v2[:]).then_inc(v_wr, 16)
            pool.dma_start(O["v_sample"][0].rearrange("b q h d -> (b q) (h d)"), vs[:]).then_inc(v_wr, 16)
            pool.wait_ge(p_o, 2 * H)
            for i in range(2):
                pool.dma_start(sct[:, i, :], I["state_conv"][0, 4 * i:4 * i + 4].rearrange("b w c -> (b w) c")).then_inc(sc_ld, 16)
            pool.memset(ub[:, :, 0:UPAD], 0.0).then_inc(ub_z, 1)

            kp = O["k_prompt"][0, 0].rearrange("t h d -> t (h d)")
            ks = O["k_sample"][0].rearrange("b q h d -> (b q) (h d)")
            for h in range(1, H, 2):
                c, slot = slice(P * (h - 1), P * (h + 1)), h // 2 % 2
                pool.wait_ge(ko_cp, h + 1)
                pool.dma_start(kp[2 * P:NP, c], ktok[0:NP - 2 * P, slot, 2, :]).then_inc(ko_wr[2 + slot], 16)
                pool.dma_start(ks[:, c], ktok[NP - 2 * P:NT - 2 * P, slot, 2, :]).then_inc(ko_wr[2 + slot], 16)

            pool.wait_ge(v_wr, 48)
            for i in range(4):
                pool.wait_ge(ko_wr[i], (16 if i < 2 else 32) * H // 4)
            pool.wait_ge(qs_dn, 1)
            pool.wait_ge(p_o, 2 * H)
            pool.wait_ge(ln_dn, H)
            pool.wait_ge(sc_cp, CT)

            def pages(dst, src, landed, used):
                def body(g):
                    for n in range(4):
                        pool.wait_ge(used, g * 4 + (n + 1))
                        pool.dma_start(dst[:, n:n + 1, :], src[bass.ds(page(g * 4 + n), 1)].rearrange("o s n -> s o n")).then_inc(landed[n], 16)
                return body

            pool.sem_inc(k_tr, 4)
            k_pages = pages(kst, cache_k, k_ld, k_tr)
            k_pages(0)
            pool.dma_start(cblk[:], I["c_blk"]).then_inc(cb_ld, 16)
            pool.dma_start(crp[:], I["c_rep"]).then_inc(cb_ld, 16)
            with pool.Fori(1, B * NPG // 4) as g:
                k_pages(g)
            pool.wait_ge(lg_done, B + 2)
            pool.sem_inc(v_used, 4)
            v_pages = pages(vst, cache_v, v_ld, v_used)
            v_pages(0)
            pool.wait_ge(u_cp, 4)
            pool.dma_start(O["conv_prompt"][0, 0], utok[0:CTX, :]).then_inc(u_wr, 16)
            for b in range(B):
                pool.dma_start(O["conv_sample"][0, b, CTX - Q:CTX], ustok[Q * b:Q * b + Q, :]).then_inc(u_wr, 16)
            pool.wait_ge(u_wr, 16 * (1 + B))
            with pool.Fori(1, B * NPG // 4) as g:
                v_pages(g)

            pool.wait_ge(ml_dn, KT)
            for i, (a, b) in enumerate([(0, 4), (4, KT)]):
                pool.dma_start(hT[:, a:b, :], xscr.rearrange("(k p) n -> p k n", p=P)[:, a:b, :]).then_inc(h_ld[i], 16)

            yp, ys = O["y_prompt"][0], O["y_sample"].rearrange("b q d -> (b q) d")

            def store(g):
                for s in range(4):
                    c = bass.ds(g * 4 * P + P * s, P)
                    pool.wait_ge(y_cp, g * 4 + (s + 3))
                    pool.dma_start(yp[:, c].rearrange("(i p) n -> p i n", p=P), ytok[:, s, 0:2, :]).then_inc(y_wr[s], 16)
                    pool.dma_start(ys[:, c], ytok[0:NS, s, 2, :]).then_inc(y_wr[s], 16)

            loop(pool, 4, store)
            for s in range(4):
                pool.wait_ge(y_wr[s], 8 * KT)
            pool.wait_ge(o_ik, 48)
            pool.wait_ge(cs_wr, 16)

        @block.scalar
        def _(act):
            ch = Chain(act, act_ch)

            def hi(G_, s, first=False):
                act.wait_ge(w_ld[s], 32 * G_ + 32)
                for r in range(4):
                    quarter(G_, s, r, first)

            def quarter(G_, s, r, first=False):
                if not first:
                    act.wait_ge(mm_done, 16 * G_ + (4 * s + r - 7))
                act.activation(WH[:, s % 2, 4 * r:4 * r + 4], RAW[:, s, 4 * r:4 * r + 4], ACT.Copy).then_inc(hi_done, 1)

            def ahead(G_, s, last=False):
                if not (last and s >= 2):
                    hi(G_ + (s + 2) // 4, (s + 2) % 4)

            def ahead_quarter(G_, s, r):
                G_, s = G_ + (s + 2) // 4, (s + 2) % 4
                if r == 0:
                    act.wait_ge(w_ld[s], 32 * G_ + 32)
                quarter(G_, s, r)

            def done(G_, s):
                act.wait_ge(mm_done, 16 * G_ + (4 * s + 4))

            def ev_wait(G_, s):
                act.wait_ge(ev[s % 2], 2 * G_ + (s // 2 + 2))

            act.wait_ge(x_ld, 80)
            act.wait_ge(pool_init, 2)
            for i, (_, n) in enumerate(XTILES):
                act.activation(xs[0:n, i, :], xtok[0:n, i, :], ACT.Square, accum_out=stat[0:n, i:i + 1]).then_inc(act_ch, 1)
            ch.start += 3
            ch.wait()
            act.activation(stat[:, 4:7], stat[:, 0:3], ACT.Sqrt, scale=1.0 / D, bias=eps[:, 0:1]).then_inc(a_sqrt, 1)
            act.wait_ge(a_rms, 1)
            for i, (_, n) in enumerate(XTILES):
                act.activation(xs[0:n, i, :], xtok[0:n, i, :], ACT.Copy, scale=stat[0:n, 8 + i:9 + i]).then_inc(a_xs, 1)
            act.wait_ge(a_prm, 1)
            banks = [TB[0], TB[1], SB[0], SB[1]]
            for k in range(KT):
                act.wait_ge(a_tr, KT + k + 1)
                act.activation(XH[:, k, :], banks[k % 4][:, 0:NT], ACT.Identity, scale=prm[:, R_GMIX + k:R_GMIX + k + 1]).then_inc(a_hi, 1)
            hi(0, 0, True)
            hi(0, 1, True)

            def iq(g):
                for s in range(4):
                    ahead(G0["iq"] + g, s)
                    done(G0["iq"] + g, s)
                    h = bass.ds(g * 4 + s, 1)
                    act.activation(iqT[:, h, :], G[s % 2][:, None, 0:SEQ], ACT.Copy)
                    for r in range(2):
                        rows = slice(64 * r, 64 * r + 64)
                        ins = act.activation(iqs[rows, :, h, r, :], G[s % 2][rows, SEQ:NQ].rearrange("p (b o q) -> p b o q", b=B, o=1), ACT.Copy)
                    ins.then_inc(ev[s % 2], 1)

            act.wait_ge(pool_zero, 1)
            loop(act, GN["iq"], iq)

            g = G0["ikiw"]
            for s in range(4):
                ahead(g, s)
                if s % 2:
                    done(g, s)
                    half = NT // 2
                    for i in range(2):
                        c = slice(half * i, half * i + half)
                        if s == 1:
                            ins = act.activation(ikT[:, c], MB[0][:, c], ACT.Copy)
                        else:
                            ins = act.activation(iwT[:, c], MB[1][0:IH, c], ACT.Copy, scale=2.0 ** -5)
                        ins.then_inc(ev[i], 1)

            act.wait_ge(d_setup, 1)
            act.activation(iktok[:, 0:2, :], TB[1][:, 0:2 * ID].rearrange("p (i d) -> p i d", i=2), ACT.Copy)
            act.activation(iktok[0:NT - 2 * P, 2, :], TB[1][0:NT - 2 * P, 2 * ID:3 * ID], ACT.Copy).then_inc(d_cpA, 1)
            act.sem_inc(d_rlA, 1)

            def pages(b, j):
                act.activation(ikb[:, j], ikst[:, bass.ds(b, 1)].rearrange("p o t d -> p (o t) d")[:, :, None, :].to_broadcast([P, NPG, 2, ID]),
                               ACT.Copy).then_inc(d_page, 1)

            def keys(b, j):
                act.wait_ge(ik_tr, b + 1)
                act.activation(ikTp[:, j, 0:512], TB[0][:], ACT.Copy).then_inc(d_cpA, 1)

            def relu(b, j):
                act.wait_ge(idx_mm, b + 1)
                act.activation(rl[:, j, 0:512], SB[0][:], ACT.Relu)
                act.activation(rl[:, j, PAST:LS], MB[0][:, 0:Q], ACT.Relu).then_inc(d_rlA, 1)

            def idx(g, last=False):
                b = g * 2
                pages(b + 1, 1)
                relu(b, 0)
                keys(b + 1, 1)
                if not last:
                    pages(b + 2, 0)
                relu(b + 1, 1)
                if not last:
                    keys(b + 2, 0)

            act.wait_ge(ik_ld, 16 * B * NPG)

            pages(0, 0)
            keys(0, 0)
            loop(act, B // 2 - 1, idx)
            idx(B // 2 - 1, True)
            for i in range(2 * IH):
                nk = keys_of(i % 2)
                act.wait_ge(pp_mm, i + 1)
                if i >= 2:
                    act.wait_ge(pp_acc, i - 1)
                act.activation(rp[:, i % 2, 0:nk], SB[i % 2][:, 0:nk], ACT.Relu).then_inc(pp_relu, 1)

            act.sem_inc(sqrt_done, 2)
            act.wait_ge(pp_acc, 2 * IH)

            def qk(g):
                def evacuate(s):
                    done(G0["qk"] + g, s)
                    act.activation(sq[:, s % 2, :], G[s % 2][:, 0:NT], ACT.Square).then_inc(sq_done, 1)
                    act.activation(QK[:, bass.ds(g * 4 + s, 1), :], G[s % 2][:, None, 0:NT], ACT.Copy).then_inc(ev[s % 2], 1)

                def root(s):
                    act.wait_ge(st_done, g * 4 + (s + 1))
                    act.wait_ge(nm_done, g * 4 + (s + 1))
                    act.activation(rt[:, s % 2, :], MB[s % 2][:, 0:NT], ACT.Sqrt, scale=1.0 / P, bias=eps[:, 0:1]).then_inc(sqrt_done, 1)

                for s in range(4):
                    ahead(G0["qk"] + g, s)
                    evacuate(s)
                    if s:
                        root(s - 1)
                root(3)

            loop(act, GN["qk"], qk)

            def v(g):
                for s in range(4):
                    ahead(G0["v"] + g, s)
                    done(G0["v"] + g, s)
                    act.wait_ge(nm_done, 2 + 2 * H)
                    act.activation(vT[:, s % 2, :], G[s % 2][:, 0:NT], ACT.Copy).then_inc(ev[s % 2], 1)

            loop(act, GN["v"], v)

            def p_soft(i):
                nk = keys_of(i // H)
                act.wait_ge(p_max, i + 1)
                act.activation(Lp[:, i % 4, 0:nk], Lp[:, i % 4, 0:nk], ACT.Exp, bias=stat[:, 16 + i % 4:17 + i % 4],
                               accum_out=stat[:, 20 + i % 4:21 + i % 4]).then_inc(p_exp, 1)

            p_soft(0)
            p_soft(1)
            for i in range(2 * H):
                if i + 2 < 2 * H:
                    p_soft(i + 2)
                act.wait_ge(p_tr, i + 1)
                if i >= 2:
                    act.wait_ge(p_pv, i - 1)
                full = i // H + 1
                act.activation(pT[:, i % 2, 0:full, :], MB[i % 2][:, 0:full * P].rearrange("p (k n) -> p k n", k=full), ACT.Copy)
                act.activation(pT[0:N_META, i % 2, full, :], MB[i % 2][0:N_META, full * P:full * P + P], ACT.Copy).then_inc(p_cp, 1)
            act.wait_ge(p_o, 2 * H)
            act.activation(qs[:], QK[:, 0:H, NP:NT], ACT.Copy).then_inc(qs_dn, 1)
            kp = O["k_prompt"][0, 0].rearrange("t h d -> t (h d)")
            for h in range(H):
                slot, c = h // 2 % 2, slice(P * (h % 2), P * (h % 2) + P)
                act.wait_ge(ko_tr, h + 1)
                if h >= 4:
                    act.wait_ge(ko_wr[slot], 16)
                    act.wait_ge(ko_wr[2 + slot], 32)
                act.activation(ktok[:, slot, 0:2, c], TB[h % 2][:, 0:2 * P].rearrange("p (i d) -> p i d", i=2), ACT.Copy)
                act.activation(ktok[0:NT - 2 * P, slot, 2, c], TB[h % 2][0:NT - 2 * P, 2 * P:3 * P], ACT.Copy).then_inc(ko_cp, 1)
                if h % 2:
                    act.wait_ge(ko_cp, h + 1)
                    act.dma_start(kp[0:2 * P, P * (h - 1):P * (h + 1)].rearrange("(i p) n -> p i n", p=P), ktok[:, slot, 0:2, :]).then_inc(ko_wr[slot], 16)
            for c in range(CT):
                act.wait_ge(sc_tr, c + 1)
                act.activation(ub[:, c, UP:UW].rearrange("p (b w) -> p b w", b=B)[:, :, 0:CTX],
                               MB[c % 2][:, 0:B * CTX].rearrange("p (b w) -> p b w", b=B), ACT.Copy).then_inc(sc_cp, 1)

            act.sem_inc(kc_A, 1)

            def cz(g):
                for s in range(4):
                    for j in range(4):
                        act.wait_ge(k_tr, g * 16 + (4 * s + j + 5))
                        act.activation(kTs[:, 0:4, :], TB[0][:].rearrange("p (h n) -> p h n", h=4), ACT.Copy).then_inc(kc_A, 1)
                        ahead_quarter(G0["cz"] + g, s, j)
                    if s % 2 == 0:
                        done(G0["cz"] + g, s)
                        act.wait_ge(ev[1], 2 * (G0["cz"] + g) + (1 + s // 2))
                        act.activation(sgt[:], G[0][:, 0:NT], ACT.Sigmoid).then_inc(ev[0], 1)

            loop(act, GN["cz"], cz)

            act.wait_ge(lg_done, B + 2)
            act.activation(uss[:],
                           ub[:, :, UP:UW].rearrange("p c (b w) -> p c b w", b=B)[:, :, :, CTX:CTX + Q], ACT.Copy).then_inc(u_s, 1)
            for i in range(2):
                act.wait_ge(u_tr, i + 1)
                act.activation(utok[0:CTX, 512 * i:512 * i + 512], TB[i][0:CTX, :], ACT.Copy).then_inc(u_cp, 1)
            for i in range(2):
                act.wait_ge(u_tr, i + 3)
                act.activation(ustok[:, 512 * i:512 * i + 512], SB[i][0:NS, :], ACT.Copy).then_inc(u_cp, 1)
            for t in range(NPG):
                act.wait_ge(x_sub, t + 1)
                act.activation(L[:, t], L[:, t], ACT.Exp).then_inc(x_exp, 1)
            act.wait_ge(x_sub, NPG + 1)
            act.activation(LN[:], LN[:], ACT.Exp).then_inc(x_exp, 1)

            act.sem_inc(os_done, 2)
            act.sem_inc(yc_done, 2)

            def ga(g):
                for s in range(4):
                    ahead(G0["ga"] + g, s)
                    done(G0["ga"] + g, s)
                    act.wait_ge(x_rs, 1)
                    act.wait_ge(u_wr, 16 * (1 + B))
                    act.activation(SGA[:, bass.ds(g * 4 + s, 1), :], G[s % 2][:, None, 0:NQ], ACT.Sigmoid).then_inc(ev[s % 2], 1)
                    if s % 2:
                        c = g * 2 + s // 2
                        act.wait_ge(v_used, c * NPG + (NPG + 4))
                        act.activation(oT[:, :, bass.ds(c * Q + SEQ, Q)], SB[s // 2][:, 0:NS].rearrange("p (h q) -> p h q", h=H), ACT.Copy).then_inc(os_done, 1)
                        act.wait_ge(cv_done, c + 1)
                        act.activation(ub[:, bass.ds(c, 1), 0:NQ], ya[:, s // 2, 0:1, :], ACT.Copy).then_inc(yc_done, 1)

            loop(act, GN["ga"], ga)

            act.wait_ge(yc_done, CT + 2)
            act.wait_ge(o_sc, 1)
            act.activation(OH[:], oT[:], ACT.Copy).then_inc(oh_dn, 1)
            for c in range(CT):
                act.wait_ge(mu_dn, c + 1)
                if c >= 2:
                    act.wait_ge(va_mm, c - 1)
                act.activation(csq[:, c % 2, :], ub[:, c, 0:NQ], ACT.Square).then_inc(cs_sq, 1)
            act.wait_ge(va_mm, CT)
            act.activation(crt[:], MB[1][:, 0:NQ], ACT.Sqrt, scale=1.0 / CC, bias=eps[:, 0:1]).then_inc(cs_rt, 1)
            for c in range(CT):
                act.wait_ge(cy_dn, c + 1)
                act.activation(ub[:, c, 0:NQ], ub[:, c, 0:NQ], ACT.Silu, scale=prm[:, R_LNG + c:R_LNG + c + 1],
                               bias=prm[:, R_LNB + c:R_LNB + c + 1]).then_inc(cs_si, 1)
            for c in range(CT):
                act.wait_ge(cs_si, c + 1)
                act.activation(CH[:, c, :], ub[:, c, 0:NQ], ACT.Copy).then_inc(ch_dn, 1)

            def merge(g):
                for s in range(4):
                    ahead(G0["merge"] + g, s)
                    if s % 2 == 0:
                        done(G0["merge"] + g, s)
                        act.activation(gbs[:, s // 2, :], G[0][:, 0:NQ], ACT.Sigmoid).then_inc(ev[0], 1)
                    else:
                        act.wait_ge(m_dn, g * 2 + (s // 2 + 1))
                        act.activation(MH[:, bass.ds(g * 2 + s // 2, 1), :], mt[:, s // 2:s // 2 + 1, :], ACT.Copy).then_inc(mh_dn, 1)

            loop(act, GN["merge"], merge)

            def out(g):
                for s in range(4):
                    ahead(G0["out"] + g, s)
                    f = g * 4 + s
                    ev_wait(G0["out"] + g, s)
                    act.activation(sq2[:, s % 2:s % 2 + 1, :], hT[:, bass.ds(f, 1), :], ACT.Square).then_inc(h_sq, 1)
                    act.activation(XH[:, bass.ds(f, 1), 0:NQ], hT[:, bass.ds(f, 1), :], ACT.Identity,
                                   scale=prm[:, bass.ds(f + R_GFFN, 1)]).then_inc(xh_dn, 1)

            loop(act, GN["out"], out)
            act.wait_ge(h_st, KT + 1)
            act.activation(rf[:], MB[0][:, 0:NQ], ACT.Sqrt, scale=1.0 / D, bias=eps[:, 0:1]).then_inc(rf_sq, 1)

            for n, (k0, m) in enumerate(PARTS):
                def gu(g):
                    for s in range(4):
                        ahead(G0[f"gu{n}"] + g, s)
                        if s % 2 == 0:
                            ev_wait(G0[f"gu{n}"] + g, s)
                            act.activation(gt[:, s // 2, :], gt[:, s // 2, :], ACT.Silu).then_inc(si_dn, 1)
                        else:
                            act.wait_ge(ac_dn, g * 2 + (k0 + s // 2 + 1))
                            act.activation(MH[:, bass.ds(g * 2 + s // 2, 1), :], at2[:, s // 2:s // 2 + 1, :], ACT.Copy).then_inc(ah_dn, 1)

                loop(act, GN[f"gu{n}"], gu)
                final = n == len(PARTS) - 1

                def by_token(g, s):
                    act.wait_ge(y_tr, g * 4 + (s + 1))
                    if not isinstance(g, int) or g:
                        act.wait_ge(y_wr[s], g * 32)
                    act.activation(ytok[:, s, 0:2, :], MB[s % 2][:, 0:2 * P].rearrange("p (i d) -> p i d", i=2), ACT.Copy)
                    act.activation(ytok[0:NS, s, 2, :], MB[s % 2][0:NS, 2 * P:3 * P], ACT.Copy).then_inc(y_cp, 1)

                def dn(g, last=False):
                    for s in range(4):
                        ahead(G0[f"dn{n}"] + g, s, last)
                        if final and s:
                            by_token(g, s - 1)
                    if final:
                        by_token(g, 3)

                if final:
                    act.sem_inc(y_cp, 2)
                    dn(0)
                    with act.Fori(1, GN[f"dn{n}"] - 1) as g:
                        dn(g)
                    dn(GN[f"dn{n}"] - 1, True)
                else:
                    loop(act, GN[f"dn{n}"], dn)

        @block.vector
        def _(dve):
            ch = Chain(dve, dve_ch)
            ch.spare = stat[0:1, 63:64]
            SC = P ** -0.5

            def lo(G_, s):
                for r in range(4):
                    quarter(G_, s, r)

            def quarter(G_, s, r):
                k = slice(4 * r, 4 * r + 4)
                dve.wait_ge(hi_done, 16 * G_ + (4 * s + r + 1))
                dve.tensor_tensor(WL[:, s % 2, k], RAW[:, s, k], WH[:, s % 2, k].bitcast(F32), ALU.subtract).then_inc(lo_done, 1)

            def ahead(G_, s, last=False):
                if not (last and s >= 2):
                    lo(G_ + (s + 2) // 4, (s + 2) % 4)

            def ahead_quarter(G_, s, r):
                quarter(G_ + (s + 2) // 4, (s + 2) % 4, r)

            def done(G_, s):
                dve.wait_ge(mm_done, 16 * G_ + (4 * s + 4))

            def ev_wait(G_, s):
                dve.wait_ge(ev[s % 2], 2 * G_ + (s // 2 + 2))

            banks = [TB[0], TB[1], SB[0], SB[1]]
            for k in range(KT):
                dve.wait_ge(a_tr, k + 1)
                dve.tensor_copy(xTs[:, k, :], banks[k % 4][:, T0C:NT]).then_inc(a_raw, 1)
                if k == 3 * KT // 4:
                    dve.wait_ge(a_sqrt, 1)
                    dve.reciprocal(stat[:, 8:11], stat[:, 4:7]).then_inc(a_rms, 1)
            dve.wait_ge(a_par, 1)
            ch.step(dve.tensor_copy(prm[:], G[0][:, 0:R_N]))
            dve.tensor_copy(wdw[:], G[1][:, 0:CT * CW].rearrange("p (c w) -> p c w", c=CT))
            ch.wait()
            dve.tensor_copy(gqk[:, 0:H], prm[:, R_QG:R_QG + 1].to_broadcast([P, H]))
            dve.tensor_copy(gqk[:, H:2 * H], prm[:, R_KG:R_KG + 1].to_broadcast([P, H])).then_inc(a_prm, 1)
            for k in range(KT):
                dve.wait_ge(a_hi, k + 1)
                dve.scalar_tensor_tensor(XL[:, k, :], banks[k % 4][:, 0:NT], prm[:, R_GMIX + k:R_GMIX + k + 1],
                                         XH[:, k, :].bitcast(F32), ALU.mult, ALU.subtract).then_inc(a_lo, 1)
            lo(0, 0)
            lo(0, 1)

            def ring(name):
                def body(g):
                    for s in range(4):
                        ahead(G0[name] + g, s)
                loop(dve, GN[name], body)

            ring("iq")
            dve.wait_ge(a_tab, 1)
            dve.tensor_copy(gsb[:], SB[0][0:H, 0:RELW])
            dve.tensor_copy(biasS[:, NPG - 1], SB[1][:, 0:Q * H].rearrange("p (q h) -> p h q", q=Q))
            for t in range(NPG - 1):
                dve.tensor_copy(biasS[:, t], SB[1][:, Q * H:Q * H + H][:, :, None].to_broadcast([P, H, Q]))
            dve.tensor_copy(biasN[:], TB[0][0:NS, 0:Q * H].rearrange("p (q h) -> p h q", q=Q)).then_inc(a_bias, 1)
            ring("ikiw")

            dve.wait_ge(d_setup, 1)
            dve.tensor_copy(iwtok[:], TB[0][:, 0:2 * IH].rearrange("p (i h) -> p i h", i=2))
            dve.wait_ge(pool_zero, 1)
            dve.tensor_tensor(IW[:, :, 0:Q], TB[0][:, 2 * IH:2 * IH + NS].rearrange("p (b q) -> p b q", b=B),
                              qm[:, None, :].to_broadcast([P, B, Q]), ALU.mult).then_inc(d_iw, 1)
            dve.sem_inc(d_cpD, 1)
            dve.sem_inc(d_rlD, 1)

            def keys(b, j):
                dve.wait_ge(ik_tr, b + 1)
                dve.tensor_copy(ikTp[:, j, 512:PAST], TB[1][:]).then_inc(d_cpD, 1)

            def relu(b, j):
                dve.wait_ge(idx_mm, b + 1)
                dve.tensor_scalar(rl[:, j, 512:PAST], SB[1][:], 0.0, None, ALU.max).then_inc(d_rlD, 1)

            def idx(g, last=False):
                b = g * 2
                relu(b, 0)
                keys(b + 1, 1)
                relu(b + 1, 1)
                if not last:
                    keys(b + 2, 0)

            keys(0, 0)
            loop(dve, B // 2 - 1, idx)
            idx(B // 2 - 1, True)
            dve.wait_ge(sum_mm, B + 3)
            for i in range(2):
                dve.tensor_copy(Ss[:, 512 * i:512 * i + 512], G[i][0:NS, :])
            ch.link(dve.tensor_tensor(Ss[:, PAST:LS], MB[1][0:NS, 0:Q], cms[:], ALU.min))
            dve.tensor_copy(Ws[:], Ss[:]).then_inc(d_ss, 1)
            for i in range(2 * IH):
                h, qt = i // 2, i % 2
                nk = keys_of(qt)
                dve.wait_ge(pp_relu, i + 1)
                if h == 0:
                    ins = dve.tensor_scalar(Sp[:, qt, 0:nk], rp[:, qt, 0:nk], iwtok[:, qt, h:h + 1], None, ALU.mult)
                else:
                    dve.wait_ge(pp_acc, i - 1)
                    ins = dve.scalar_tensor_tensor(Sp[:, qt, 0:nk], rp[:, qt, 0:nk], iwtok[:, qt, h:h + 1], Sp[:, qt, 0:nk],
                                                   ALU.mult, ALU.add)
                ins.then_inc(pp_acc, 1)
            dve.wait_ge(pp_acc, 2 * IH)
            for qt in range(2):
                nk = keys_of(qt)
                ch.link(dve.tensor_tensor(Sp[:, qt, 0:nk], Sp[:, qt, 0:nk], cmp_[:, qt, 0:nk], ALU.min))
                ch.link(dve.tensor_copy(Wp[:, qt, 0:nk], Sp[:, qt, 0:nk]))

            def take8(best, scores):
                best8(best, scores)
                taken8(best, scores)

            def best8(best, scores):
                ch.rest()
                ch.step(dve.max(best, scores))

            def taken8(best, scores):
                ch.rest()
                ch.step(dve.match_replace(scores, best, scores, TAKEN))

            dve.sem_inc(nm_done, 2)

            def qk(g):
                def norm(s):
                    h = bass.ds(g * 4 + s, 1)
                    dve.wait_ge(sqrt_done, g * 4 + (s + 3))
                    ch.link(dve.reciprocal(rt[:, s % 2, :], rt[:, s % 2, :]))
                    dve.scalar_tensor_tensor(QK[:, h, :], QK[:, h, :], gqk[:, h], rt[:, s % 2:s % 2 + 1, :],
                                             ALU.mult, ALU.mult).then_inc(nm_done, 1)

                ch.loop(g, 20)
                for s in range(4):
                    ahead(G0["qk"] + g, s)
                    take8(m8s[:], Ws[:])
                    take8(m8p[:, s % 2, :], Wp[:, s % 2, 0:keys_of(s % 2)])
                    if s:
                        norm(s - 1)
                norm(3)

            loop(dve, GN["qk"], qk)
            ch.end(GN["qk"])

            for qt in range(2):
                nk = keys_of(qt)
                ch.link(dve.tensor_tensor(Wp[:, qt, 0:nk], Wp[:, qt, 0:nk], Sp[:, qt, 0:nk], ALU.is_equal))
                dve.tensor_scalar(Wp[:, qt, 0:nk], Wp[:, qt, 0:nk], NEG / SC, None, ALU.mult).then_inc(p_mask, 1)

            dve.sem_inc(vk_done, 2)
            dve.wait_ge(o_ik, 48)

            def v(g):
                def copy(s):
                    c = bass.ds(g * 4 * P + P * s, P)
                    dve.wait_ge(vtr, g * 4 + (s + 1))
                    dve.tensor_copy(vtok[:, :, c], MB[s % 2][:, 0:2 * P].rearrange("p (i d) -> p i d", i=2))
                    dve.tensor_copy(v2[:, c], MB[s % 2][0:N_META, 2 * P:3 * P])
                    dve.tensor_copy(vs[:, c], MB[s % 2][0:NS, 3 * P:4 * P]).then_inc(vk_done, 1)

                ch.loop(g, 8)
                for s in range(4):
                    ahead(G0["v"] + g, s)
                    take8(m8s[:], Ws[:])
                    if s:
                        copy(s - 1)
                copy(3)

            loop(dve, GN["v"], v)
            ch.end(GN["v"])

            sbank = [SB[0], SB[1], TB[0], TB[1]]

            def p_logits(i):
                qt, h = i // H, i % H
                nk, z0 = keys_of(qt), P * (1 - qt)
                row = Lp[:, i % 4, 0:nk]
                dve.wait_ge(p_qk, i + 1)
                if i == 0:
                    dve.wait_ge(tb_ld, 16)
                if i >= 4:
                    dve.wait_ge(p_tr, i - 3)
                dve.scalar_tensor_tensor(row, sbank[i % 4][:, 0:nk], SC, Tb[:, h, z0:z0 + nk], ALU.mult, ALU.add).then_inc(p_lg, 1)
                dve.wait_ge(p_lg, i + 1)
                dve.tensor_reduce(stat[:, 16 + i % 4:17 + i % 4], row, AX, ALU.max, negate=True).then_inc(p_max, 1)

            def p_norm(i):
                nk = keys_of(i // H)
                r = stat[:, 20 + i % 4:21 + i % 4]
                dve.wait_ge(p_exp, i + 1)
                ch.link(dve.reciprocal(r, r))
                dve.tensor_scalar(Lp[:, i % 4, 0:nk], Lp[:, i % 4, 0:nk], r, None, ALU.mult).then_inc(p_nrm, 1)

            def p_out(i):
                qt, h = i // H, i % H
                dve.wait_ge(p_pv, i + 1)
                dve.tensor_copy(oT[:, h, qt * P:qt * P + P], MB[i % 2][:, 3 * P:4 * P]).then_inc(p_o, 1)

            p_logits(0)
            p_logits(1)
            for i in range(2 * H):
                if i + 2 < 2 * H:
                    p_logits(i + 2)
                if i >= 2:
                    p_out(i - 2)
                p_norm(i)
            p_out(2 * H - 2)
            p_out(2 * H - 1)
            dve.wait_ge(ln_mm, H)
            for h in range(H):
                dve.scalar_tensor_tensor(LN[:, :, h, :], SB[0][0:NS, NS * h:NS * h + NS].rearrange("p (b q) -> p b q", b=B), SC,
                                         biasN[:, h:h + 1, :].to_broadcast([NS, B, Q]), ALU.mult, ALU.add).then_inc(ln_dn, 1)

            dve.sem_inc(kc_D, 1)
            dve.sem_inc(lg_done, 2)
            dve.wait_ge(ub_z, 1)

            def cz(g):
                ch.loop(g, 4)
                for s in range(4):
                    G_, b = G0["cz"] + g, g * 2 + s // 2
                    c = bass.ds(b, 1)
                    for j in range(4):
                        dve.wait_ge(k_tr, g * 16 + (4 * s + j + 5))
                        dve.tensor_copy(kTs[:, 4:8, :], TB[1][:].rearrange("p (h n) -> p h n", h=4)).then_inc(kc_D, 1)
                        ahead_quarter(G_, s, j)
                        if s % 2 == 0 and j == 0:
                            best8(m8s[:], Ws[:])
                        if s % 2 == 0 and j == 2:
                            taken8(m8s[:], Ws[:])
                    if s % 2 == 0:
                        continue
                    ev_wait(G_, s - 1)
                    done(G_, s)
                    dve.tensor_tensor(ub[:, c, UPAD:UP], G[1][:, None, 0:NP], sgt[:, None, 0:NP], ALU.mult)
                    dve.tensor_tensor(ub[:, c, UP:UW].rearrange("p o (b w) -> p (o b) w", b=B)[:, :, CTX:CTX + Q],
                                      G[1][:, NP:NT].rearrange("p (b q) -> p b q", b=B), sgt[:, NP:NT].rearrange("p (b q) -> p b q", b=B),
                                      ALU.mult).then_inc(ev[1], 1)
                    dve.wait_ge(kq_done, b + 1)
                    dve.scalar_tensor_tensor(L[:, :, c, :].rearrange("p t o x -> p t (o x)"), SB[s // 2][:].rearrange("p (t x) -> p t x", t=NPG), SC,
                                             biasS[:].rearrange("p t h q -> p t (h q)"), ALU.mult, ALU.add).then_inc(lg_done, 1)

            loop(dve, GN["cz"], cz)
            ch.end(GN["cz"])

            ch.wait()
            dve.wait_ge(lg_done, B + 2)
            dve.wait_ge(ln_dn, H)
            dve.tensor_tensor(Ws[:], Ws[:], Ss[:], ALU.is_equal).then_inc(x_e, 1)
            dve.wait_ge(x_tr, 1)
            ch.step(dve.tensor_scalar(MS[:], TB[0][:].rearrange("p (t x) -> p t x", t=NPG), NEG, None, ALU.mult))
            dve.tensor_scalar(e8[:], TB[1][0:Q, 0:NS], NEG, None, ALU.mult).then_inc(x_m, 1)
            ch.wait()
            for t in range(NPG):
                row = L[:, t].rearrange("p b (h q) -> p b h q", h=H)
                ch.step(dve.tensor_tensor(row, row, MS[:, t, :].rearrange("p (b o q) -> p b o q", b=B, o=1).to_broadcast([P, B, H, Q]), ALU.add))
            dve.wait_ge(x_rep, 1)
            dve.wait_ge(cb_ld, 32)
            ch.link(dve.tensor_tensor(MN[:], MB[0][0:NS, 0:NS], cblk[:], ALU.add))
            dve.tensor_tensor(LN[:], LN[:], MN[:].rearrange("p (b o q) -> p b o q", b=B, o=1).to_broadcast([NS, B, H, Q]), ALU.add).then_inc(x_mn, 1)
            dve.tensor_reduce(mx[:].rearrange("p i x -> p (i x)"), L[:].rearrange("p t b x -> p (b x) t"), AX, ALU.max).then_inc(x_mx, 1)
            dve.wait_ge(x_mt, 1)
            ch.step(dve.tensor_reduce(stat[:, 24:28], SB[0][:].rearrange("p (i x) -> p i x", i=4), AX, ALU.max))
            ch.link(dve.tensor_reduce(stat[:, 28:32], SB[1][:, 0:4 * NS].rearrange("p (i x) -> p i x", i=4), AX, ALU.max))
            ch.link(dve.tensor_tensor(stat[:, 32:36], stat[:, 24:28], stat[:, 28:32], ALU.max))
            for i in range(4):
                ins = dve.tensor_scalar(dg[:, i, :], ident[:], stat[:, 32 + i:33 + i], None, ALU.mult)
            ins.then_inc(x_dg, 1)
            dve.wait_ge(x_bc, 1)
            for t in range(NPG):
                row = L[:, t].rearrange("p b x -> p (b x)")
                dve.tensor_tensor(row, row, MB[1][:], ALU.subtract).then_inc(x_sub, 1)
            row = LN[:].rearrange("p b h q -> p (b h q)")
            dve.wait_ge(x_mn, 1)
            dve.tensor_tensor(row, row, MB[1][0:NS, :], ALU.subtract).then_inc(x_sub, 1)
            dve.wait_ge(x_exp, NPG)
            dve.tensor_reduce(mx[:].rearrange("p i x -> p (i x)"), L[:].rearrange("p t b x -> p (b x) t"), AX, ALU.add).then_inc(x_sm, 1)
            dve.wait_ge(x_den, 1)
            dve.reciprocal(rS[:].rearrange("p b h q -> p (b h q)"), TB[0][:]).then_inc(x_rs, 1)

            taps = (CW + 1) // 2

            def ga(g):
                ch.loop(g, 4 * CW)
                for s in range(4):
                    c = g * 2 + s // 2
                    one = ub[:, bass.ds(c, 1), :]
                    first = 0 if s % 2 == 0 else taps
                    for w in range(first, taps if s % 2 == 0 else CW):
                        if (w - first) % (taps // 4) == 0:
                            ahead_quarter(G0["ga"] + g, s, (w - first) // (taps // 4))
                        z = ya[:, s // 2, w % 2, :]
                        zs = z[:, SEQ:NQ].rearrange("p (b q) -> p b q", b=B)
                        xp = one[:, :, w:w + SEQ].rearrange("p o n -> p (o n)")
                        xq = one[:, :, UP:UW].rearrange("p o (b w) -> p (o b) w", b=B)[:, :, w:w + Q]
                        tap = wdw[:].rearrange("p c w -> p (c w)")[:, bass.ds(c * CW + w, 1)]
                        if w == 0:
                            bias = prm[:, bass.ds(c + R_BDW, 1)]
                            dve.wait_ge(yc_done, c + 1)
                            ch.step(dve.tensor_scalar(z[:, 0:SEQ], xp, tap, bias, ALU.mult, ALU.add))
                            ch.step(dve.tensor_scalar(zs, xq, tap, bias, ALU.mult, ALU.add))
                        elif w == 1:
                            ch.step(dve.tensor_scalar(z[:, 0:SEQ], xp, tap, None, ALU.mult))
                            ch.step(dve.tensor_scalar(zs, xq, tap, None, ALU.mult))
                        else:
                            ch.wait_back(3)
                            ch.step(dve.scalar_tensor_tensor(z[:, 0:SEQ], xp, tap, z[:, 0:SEQ], ALU.mult, ALU.add))
                            ch.wait_back(3)
                            ch.step(dve.scalar_tensor_tensor(zs, xq, tap, zs, ALU.mult, ALU.add))
                    if s % 2:
                        ch.wait()
                        z = ya[:, s // 2]
                        dve.tensor_tensor(z[:, 0, :], z[:, 0, :], z[:, 1, :], ALU.add).then_inc(cv_done, 1)

            loop(dve, GN["ga"], ga)

            dve.wait_ge(np_mm, 1)
            dve.wait_ge(os_done, B + 2)
            o = oT[:, :, SEQ:NQ]
            ch.end(GN["ga"])
            ch.link(dve.tensor_tensor(o, o, TB[0][:].rearrange("p (h x) -> p h x", h=H), ALU.add))
            o = o.rearrange("p h (b q) -> p h b q", b=B)
            dve.tensor_tensor(o, o, rS[:].rearrange("p b h q -> p h b q"), ALU.mult).then_inc(o_sc, 1)
            dve.wait_ge(oh_dn, 1)
            dve.tensor_tensor(OL[:], oT[:], OH[:].bitcast(F32), ALU.subtract).then_inc(ol_dn, 1)
            dve.wait_ge(mu_mm, 1)
            for c in range(CT):
                dve.scalar_tensor_tensor(ub[:, c, 0:NQ], MB[0][:, 0:NQ], -1.0 / CC, ub[:, c, 0:NQ], ALU.mult, ALU.add).then_inc(mu_dn, 1)
            dve.wait_ge(cs_rt, 1)
            ch.link(dve.reciprocal(crt[:], crt[:]))
            dve.wait_ge(mu_dn, CT)
            for c in range(CT):
                dve.tensor_tensor(ub[:, c, 0:NQ], ub[:, c, 0:NQ], crt[:], ALU.mult).then_inc(cy_dn, 1)
            for c in range(CT):
                dve.wait_ge(ch_dn, c + 1)
                dve.tensor_tensor(CL[:, c, :], ub[:, c, 0:NQ], CH[:, c, :].bitcast(F32), ALU.subtract).then_inc(cl_dn, 1)

            def merge(g):
                ch.loop(g, 2)
                for s in range(4):
                    ahead(G0["merge"] + g, s)
                    if s % 2 == 0:
                        continue
                    G_, f, z = G0["merge"] + g, g * 2 + s // 2, mt[:, s // 2:s // 2 + 1, :]
                    done(G_, s)
                    ch.step(dve.tensor_tensor(z, G[1][:, None, 0:NQ], SGA[:, bass.ds(f, 1), :], ALU.mult))
                    ev_wait(G_, s - 1)
                    dve.tensor_tensor(mu_[:], MB[s // 2][:, 0:NQ], gbs[:, s // 2, :], ALU.mult).then_inc(ev[1], 1)
                    dve.wait_ge(ev[1], 2 * G_ + (s // 2 + 2))
                    ch.wait()
                    dve.tensor_tensor(z, z, mu_[:, None, :], ALU.add).then_inc(m_dn, 1)
                    dve.wait_ge(mh_dn, f + 1)
                    dve.tensor_tensor(ML[:, bass.ds(f, 1), :], z, MH[:, bass.ds(f, 1), :].bitcast(F32), ALU.subtract).then_inc(ml_dn, 1)

            loop(dve, GN["merge"], merge)
            ch.end(GN["merge"])


            def out(g):
                for s in range(4):
                    G_, f = G0["out"] + g, bass.ds(g * 4 + s, 1)
                    ahead(G_, s)
                    done(G_, s)
                    dve.tensor_tensor(hT[:, f, :], G[s % 2][:, None, 0:NQ], hT[:, f, :], ALU.add).then_inc(ev[s % 2], 1)
                    dve.wait_ge(xh_dn, g * 4 + (s + 1))
                    dve.scalar_tensor_tensor(XL[:, f, 0:NQ], hT[:, f, :], prm[:, bass.ds(g * 4 + (s + R_GFFN), 1)],
                                             XH[:, f, 0:NQ].bitcast(F32), ALU.mult, ALU.subtract).then_inc(xl_dn, 1)

            dve.wait_ge(h_ld[0], 16)
            out(0)
            dve.wait_ge(h_ld[1], 16)
            with dve.Fori(1, GN["out"]) as g:
                out(g)
            dve.wait_ge(rf_sq, 1)
            dve.reciprocal(rf[:], rf[:]).then_inc(rf_dn, 1)
            dve.wait_ge(rf_dn, 1)

            for n, (k0, m) in enumerate(PARTS):
                def gu(g):
                    for s in range(4):
                        G_, f = G0[f"gu{n}"] + g, g * 2 + s // 2
                        ahead(G_, s)
                        done(G_, s)
                        if s % 2 == 0:
                            dve.tensor_tensor(gt[:, s // 2, :], G[0][:, 0:NQ], rf[:], ALU.mult).then_inc(ev[0], 1)
                            continue
                        dve.tensor_tensor(ut[:], G[1][:, 0:NQ], rf[:], ALU.mult).then_inc(ev[1], 1)
                        dve.wait_ge(ev[1], 2 * G_ + (s // 2 + 2))
                        dve.wait_ge(si_dn, f + (k0 + 1))
                        dve.tensor_tensor(at2[:, s // 2, :], gt[:, s // 2, :], ut[:], ALU.mult).then_inc(ac_dn, 1)
                        dve.wait_ge(ah_dn, f + (k0 + 1))
                        dve.tensor_tensor(ML[:, bass.ds(f, 1), :], at2[:, s // 2:s // 2 + 1, :], MH[:, bass.ds(f, 1), :].bitcast(F32),
                                          ALU.subtract).then_inc(al_dn, 1)

                loop(dve, GN[f"gu{n}"], gu)
                final = n == len(PARTS) - 1

                def dn(g, last=False):
                    for s in range(4):
                        G_, f = G0[f"dn{n}"] + g, bass.ds(g * 4 + s, 1)
                        ahead(G_, s, last)
                        done(G_, s)
                        to = at2[:, s % 2:s % 2 + 1, :] if final else hT[:, f, :]
                        dve.tensor_tensor(to, G[s % 2][:, None, 0:NQ], hT[:, f, :], ALU.add).then_inc(ev[s % 2], 1)

                if final:
                    loop(dve, GN[f"dn{n}"] - 1, dn)
                    dn(GN[f"dn{n}"] - 1, True)
                else:
                    loop(dve, GN[f"dn{n}"], dn)

        @block.tensor
        def _(pe):
            def tr(out, src):
                n = src.shape[0]
                return pe.transpose(out, src, ident[0:n, 0:n])

            def mm(out, lhsT, rhs, start=True, stop=True):
                return pe.matmul(out, lhsT, rhs, start=start, stop=stop, skip_group_check=True)

            def split_mm(out, s, k, hi, lo, start, stop):
                pe.matmul(out, WH[:, s % 2, k], hi, start=start, stop=False)
                pe.matmul(out, WH[:, s % 2, k], lo, start=False, stop=False)
                return pe.matmul(out, WL[:, s % 2, k], hi, start=False, stop=stop)

            def ready(G_, s):
                pe.wait_ge(ev[s % 2], 2 * G_ + (s // 2 + 1))

            def products(G_, s, tiles, kt, product):
                for k in tiles:
                    if k % 4 == 0:
                        whole = k + 4 >= kt
                        pe.wait_ge(lo_done, 16 * G_ + (4 * s + (4 if whole else k // 4 + 1)))
                    ins = product(k)
                    if k == kt - 1:
                        ins.then_inc(mm_done, 4 - k // 4)
                    elif k % 4 == 3:
                        ins.then_inc(mm_done, 1)

            def unit(G_, s, n, hi, lo, kt=KT, ready_sem=None, ready_from=0):
                ready(G_, s)

                def product(k):
                    if ready_sem is not None and s == 0 and k % 4 == 0:
                        pe.wait_ge(ready_sem, ready_from + min(k + 4, kt))
                    return split_mm(G[s % 2][:, 0:n], s, k, hi(k), lo(k), k == 0, k == kt - 1)

                products(G_, s, range(kt), kt, product)

            def x_all(G_, s):
                unit(G_, s, NT, lambda k: XH[:, k, :], lambda k: XL[:, k, :])

            def x_quarter(G_, s, r, first_col=0):
                if r == 0:
                    ready(G_, s)
                products(G_, s, range(4 * r, 4 * r + 4), KT,
                         lambda k: split_mm(G[s % 2][:, 0:NT - first_col], s, k, XH[:, k, first_col:NT], XL[:, k, first_col:NT], k == 0, k == KT - 1))

            def x_out(G_, s):
                unit(G_, s, NQ, lambda k: XH[:, k, T0C:NT], lambda k: XL[:, k, T0C:NT])

            def lagged(G_, main, side):
                for s in range(4):
                    main(G_, s)
                    if s:
                        side(s - 1)
                side(3)

            def lagged_all(n, main, side):
                def body(g, first=False):
                    for s in range(4):
                        main(g, s)
                        if s:
                            side(g, s - 1)
                        elif not first:
                            side(g - 1, 3)

                body(0, True)
                with pe.Fori(1, n) as g:
                    body(g)
                side(n - 1, 3)

            banks = [TB[0], TB[1], SB[0], SB[1]]

            def turn_x(src, k):
                for i, (t, n) in enumerate(XTILES):
                    ins = tr(banks[k % 4][:, t:t + n], src[0:n, i, P * k:P * k + P])
                ins.then_inc(a_tr, 1)

            pe.wait_ge(id_ld, 16)
            pe.wait_ge(x_ld, 80)
            for k in range(KT):
                if k >= 4:
                    pe.wait_ge(a_raw, k - 3)
                turn_x(xtok, k)
            pe.wait_ge(pool_init, 2)
            pe.wait_ge(c_ld, 160)
            tr(G[0][:, 0:R_N], prow[:])
            for c in range(CT):
                ins = tr(G[1][:, CW * c:CW * c + CW], wrow[:, P * c:P * c + P])
            ins.then_inc(a_par, 1)
            pe.wait_ge(a_xs, 3)
            for k in range(KT):
                if k < 4:
                    pe.wait_ge(a_raw, KT - 3 + k)
                else:
                    pe.wait_ge(a_lo, k - 3)
                turn_x(xs, k)
            pe.wait_ge(a_prm, 1)

            def iq(g):
                for s in range(4):
                    x_out(G0["iq"] + g, s)

            loop(pe, GN["iq"], iq)
            pe.wait_ge(a_lo, KT)
            mm(SB[0][0:H, 0:RELW], relx[:], oh[:, OH_G:OH_G + RELW])
            for q in range(Q):
                mm(SB[1][:, H * q:H * q + H], oh[:, OH_T7 + P * q:OH_T7 + P * q + P], relx[:])
                mm(TB[0][0:NS, H * q:H * q + H], oh[:, OH_NEW + NS * q:OH_NEW + NS * q + NS], relx[:])
            mm(SB[1][:, Q * H:Q * H + H], oh[:, OH_FAR:OH_FAR + P], relx[:]).then_inc(a_tab, 1)
            for s in range(4):
                ready(G0["ikiw"], s)

                def product(k):
                    x = 8 * (s % 2) + k
                    return split_mm(MB[s // 2][:, 0:NT], s, k, XH[:, x, :], XL[:, x, :], x == 0, x == KT - 1)

                products(G0["ikiw"], s, range(8), 8, product)

            for s in range(2):
                pe.wait_ge(ev[s], 2 * (G0["ikiw"] + 1) + 1)
            pe.wait_ge(a_bias, 1)
            for qt in range(2):
                tr(TB[0][:, IH * qt:IH * qt + IH], iwT[:, T0C + P * qt:T0C + P * qt + P])
            mm(TB[0][:, 2 * IH:2 * IH + NS], esel[:], iwT[:, NP:NT])
            for i, (t, n) in enumerate(XTILES):
                ins = tr(TB[1][0:n, ID * i:ID * i + ID], ikT[0:ID, t:t + n])
            ins.then_inc(d_setup, 1)
            sums = [G[0][0:NS, :], G[1][0:NS, :], MB[1][0:NS, 0:Q]]

            def zero(out, start):
                n = out.shape[1]
                return mm(out, zer[:, 0:out.shape[0]], biasS[:].rearrange("p t h q -> p (t h q)")[:, 0:n], start, not start)

            for out in sums:
                zero(out, True)

            def keys(b, j):
                pe.wait_ge(d_page, b + 1)
                pe.wait_ge(d_iw, 1)
                pe.wait_ge(d_cpA, b + 1)
                pe.wait_ge(d_cpD, b + 1)
                for t in range(NPG):
                    ins = tr(TB[t // 4][:, P * (t % 4):P * (t % 4) + P], ikb[:, j, t, :, :].rearrange("p r d -> p (r d)"))
                ins.then_inc(ik_tr, 1)

            def scores(b, j):
                pe.wait_ge(d_stage, b + 1)
                pe.wait_ge(d_cpA, b + 2)
                pe.wait_ge(d_cpD, b + 2)
                pe.wait_ge(d_rlA, b + 1)
                pe.wait_ge(d_rlD, b + 1)
                mm(SB[0][:], iqb[:, j, :], ikTp[:, j, 0:512])
                mm(SB[1][:], iqb[:, j, :], ikTp[:, j, 512:PAST])
                mm(MB[0][:, 0:Q], iqb[:, j, :], ikT[:, bass.ds(b * Q + NP, Q)]).then_inc(idx_mm, 1)

            def total(b, j):
                pe.wait_ge(d_rlA, b + 2)
                pe.wait_ge(d_rlD, b + 2)
                mm(sums[0], iwb[:, j, :], rl[:, j, 0:512], False, False)
                mm(sums[1], iwb[:, j, :], rl[:, j, 512:PAST], False, False)
                mm(sums[2], iwb[:, j, :], rl[:, j, PAST:LS], False, False).then_inc(sum_mm, 1)

            def idx(g, last=False):
                b = g * 2
                scores(b, 0)
                keys(b + 1, 1)
                total(b, 0)
                scores(b + 1, 1)
                if not last:
                    keys(b + 2, 0)
                total(b + 1, 1)

            keys(0, 0)
            loop(pe, B // 2 - 1, idx)
            idx(B // 2 - 1, True)
            for out in sums:
                ins = zero(out, False)
            ins.then_inc(sum_mm, 1)
            for i in range(2 * IH):
                h, qt = i // 2, i % 2
                nk = keys_of(qt)
                rows = slice(ID * (h % 2), ID * (h % 2) + ID)
                if i >= 2:
                    pe.wait_ge(pp_relu, i - 1)
                mm(SB[i % 2][:, 0:nk], iqT[rows, h // 2, P * qt:P * qt + P], ikT[rows, 0:nk]).then_inc(pp_mm, 1)
                if i == 3:
                    pe.wait_ge(d_ss, 1)
                if i % 4 == 3:
                    x_quarter(G0["qk"], i // 16, i // 4 % 4)

            def qk(g, multiplied=0):
                def squares(s):
                    pe.wait_ge(sq_done, g * 4 + (s + 1))
                    pe.wait_ge(sqrt_done, g * 4 + (s + 1))
                    mm(MB[s % 2][:, 0:NT], ones[:], sq[:, s % 2, :]).then_inc(st_done, 1)

                lagged(G0["qk"] + g, lambda G_, s: x_all(G_, s) if s >= multiplied else None, squares)

            qk(0, 2)
            with pe.Fori(1, GN["qk"]) as g:
                qk(g)
            def v_by_token(g, s):
                pe.wait_ge(ev[s % 2], 2 * (G0["v"] + g) + (s // 2 + 2))
                pe.wait_ge(vk_done, g * 4 + (s + 1))
                pe.wait_ge(sqrt_done, 2 + 2 * H)
                for i, (t, n) in enumerate([(0, P), (P, P), (2 * P, N_META), (NP, NS)]):
                    ins = tr(MB[s % 2][0:n, P * i:P * i + P], vT[:, s % 2, t:t + n])
                ins.then_inc(vtr, 1)

            lagged_all(GN["v"], lambda g, s: x_all(G0["v"] + g, s), v_by_token)

            pe.wait_ge(nm_done, 2 + 2 * H)
            pe.wait_ge(pp_relu, 2 * IH)
            sbank = [SB[0], SB[1], TB[0], TB[1]]

            def p_logits(i):
                qt, h = i // H, i % H
                if i >= 4:
                    pe.wait_ge(p_lg, i - 3)
                out = sbank[i % 4][:, 0:keys_of(qt)]
                mm(out, QK[:, h, T0C + P * qt:T0C + P * qt + P], QK[:, H + h, 0:keys_of(qt)], True, False)
                mm(out, ident[:], Wp[:, qt, 0:keys_of(qt)], False, True).then_inc(p_qk, 1)

            def p_turn(i):
                full = i // H + 1
                pe.wait_ge(p_nrm, i + 1)
                if i >= 2:
                    pe.wait_ge(p_cp, i - 1)
                    pe.wait_ge(p_o, i - 1)
                for k in range(full):
                    tr(MB[i % 2][:, P * k:P * k + P], Lp[:, i % 4, P * k:P * k + P])
                tr(MB[i % 2][0:N_META, P * full:P * full + P], Lp[:, i % 4, P * full:P * full + N_META]).then_inc(p_tr, 1)

            def p_values(i):
                full, h = i // H + 1, i % H
                c = slice(P * h, P * h + P)
                out = MB[i % 2][:, 3 * P:4 * P]
                pe.wait_ge(p_cp, i + 1)
                for k in range(full):
                    mm(out, vtok[:, k, c], pT[:, i % 2, k, :], k == 0, False)
                last = vtok[0:N_META, 1, c] if full == 1 else v2[:, c]
                mm(out, last, pT[0:N_META, i % 2, full, :], False, True).then_inc(p_pv, 1)

            pe.wait_ge(p_mask, 2)
            for i in range(3):
                p_logits(i)
            pe.wait_ge(vk_done, 2 + H)
            for i in range(2 * H):
                if i + 3 < 2 * H:
                    p_logits(i + 3)
                p_turn(i)
                if i:
                    p_values(i - 1)
            p_values(2 * H - 1)
            pe.wait_ge(p_lg, 2 * H)
            for h in range(H):
                if h >= 2:
                    pe.wait_ge(ko_cp, h - 1)
                for i, (t, n) in enumerate(XTILES):
                    ins = tr(TB[h % 2][0:n, P * i:P * i + P], QK[:, H + h, t:t + n])
                ins.then_inc(ko_tr, 1)
                mm(SB[0][0:NS, NS * h:NS * h + NS], QK[:, H + h, NP:NT], QK[:, h, NP:NT]).then_inc(ln_mm, 1)
            pe.wait_ge(sc_ld, 32)
            pe.wait_ge(p_cp, 2 * H)
            for c in range(CT):
                if c >= 2:
                    pe.wait_ge(sc_cp, c - 1)
                for i in range(2):
                    ins = tr(MB[c % 2][:, 4 * CTX * i:4 * CTX * i + 4 * CTX], sct[:, i, P * c:P * c + P])
                ins.then_inc(sc_tr, 1)

            pe.wait_ge(p_o, 2 * H)
            pe.wait_ge(ko_cp, H)
            pe.wait_ge(ln_dn, H)
            pe.wait_ge(qs_dn, 1)

            def cz(g):
                for s in range(4):
                    G_, b = G0["cz"] + g, g * 2 + s // 2
                    for j in range(4):
                        n, t = g * 16 + (4 * s + j), 4 * (s % 2) + j
                        pe.wait_ge(k_ld[j], g * 64 + 16 * (s + 1))
                        pe.wait_ge(kc_A, n + 1)
                        pe.wait_ge(kc_D, n + 1)
                        for h in range(H):
                            ins = tr(TB[h // 4][:, P * (h % 4):P * (h % 4) + P], kst[:, j, P * h:P * h + P])
                        ins.then_inc(k_tr, 1)
                        x_quarter(G_, s, j)
                        pe.wait_ge(kc_A, n + 2)
                        pe.wait_ge(kc_D, n + 2)
                        if t == 0:
                            pe.wait_ge(lg_done, b + 1)
                        for h in range(H):
                            ins = mm(SB[s // 2][:, NS * t + Q * h:NS * t + Q * h + Q], kTs[:, h, :], qs[:, h, bass.ds(b * Q, Q)],
                                     t == 0 and h == 0, t == NPG - 1 and h == H - 1)
                    if s % 2:
                        ins.then_inc(kq_done, 1)

            loop(pe, GN["cz"], cz)

            for s in range(2):
                pe.wait_ge(ev[s], 2 * G0["ga"] + 1)
            pe.wait_ge(lg_done, B + 2)
            pe.wait_ge(u_s, 1)
            for i in range(4):
                for c in range(4):
                    ct = 4 * (i % 2) + c
                    src = ub[:, ct, UP - CTX:UP] if i < 2 else uss[:, ct].rearrange("p b q -> p (b q)")
                    out = TB[i][0:CTX, P * c:P * c + P] if i < 2 else SB[i - 2][0:NS, P * c:P * c + P]
                    ins = tr(out, src)
                ins.then_inc(u_tr, 1)
            pe.wait_ge(u_cp, 2)
            pe.wait_ge(x_e, 1)
            for t in range(NPG):
                tr(TB[0][:, NS * t:NS * t + NS], Ws[:, PAGE * t:PAGE * t + PAGE])
            tr(TB[1][0:Q, 0:NS], Ws[:, PAST:LS]).then_inc(x_tr, 1)
            pe.wait_ge(x_m, 1)
            pe.wait_ge(cb_ld, 32)
            mm(MB[0][0:NS, 0:NS], crp[:], e8[:]).then_inc(x_rep, 1)
            pe.wait_ge(x_mx, 1)
            pe.wait_ge(x_mn, 1)
            pe.wait_ge(u_cp, 4)
            for i in range(4):
                tr(SB[0][:, P * i:P * i + P], mx[:, i, :])
                ins = tr(SB[1][:, NS * i:NS * i + NS], LN[:].rearrange("p b h q -> p (b h q)")[:, P * i:P * i + P])
            ins.then_inc(x_mt, 1)
            pe.wait_ge(x_dg, 1)
            mm(MB[1][:], ones[:], dg[:].rearrange("p i x -> p (i x)")).then_inc(x_bc, 1)
            pe.wait_ge(x_sm, 1)
            pe.wait_ge(x_exp, NPG + 1)
            mm(TB[0][:], ones[:], mx[:].rearrange("p i x -> p (i x)"), True, False)
            mm(TB[0][:], ones[0:NS, :], LN[:].rearrange("p b h q -> p (b h q)"), False, True).then_inc(x_den, 1)
            pe.wait_ge(x_rs, 1)

            def ga(g):
                for s in range(4):
                    G_, b = G0["ga"] + g, g * 2 + s // 2
                    for j in range(4):
                        n, t = g * 16 + (4 * s + j), 4 * (s % 2) + j
                        x_quarter(G_, s, j, T0C)
                        pe.wait_ge(v_ld[j], g * 64 + 16 * (s + 1))
                        if t == 0:
                            pe.wait_ge(os_done, b + 1)
                        for h in range(H):
                            ins = mm(SB[s // 2][:, Q * h:Q * h + Q], vst[:, j, P * h:P * h + P], L[:, t, bass.ds(b, 1), Q * h:Q * h + Q].rearrange("p o q -> p (o q)"),
                                     t == 0 and h == 0, t == NPG - 1 and h == H - 1)
                        ins.then_inc(v_used, 1)

            loop(pe, GN["ga"], ga)

            for h in range(H):
                ins = mm(TB[0][:, NS * h:NS * h + NS], vs[:, P * h:P * h + P], LN[:, :, h, :])
            ins.then_inc(np_mm, 1)
            pe.wait_ge(yc_done, CT + 2)
            for c in range(CT):
                ins = mm(MB[0][:, 0:NQ], ones[:], ub[:, c, 0:NQ], c == 0, c == CT - 1)
            ins.then_inc(mu_mm, 1)
            for c in range(CT):
                pe.wait_ge(cs_sq, c + 1)
                mm(MB[1][:, 0:NQ], ones[:], csq[:, c % 2, :], c == 0, c == CT - 1).then_inc(va_mm, 1)

            def merge(g):
                for s in range(4):
                    G_ = G0["merge"] + g
                    if s % 2 == 0:
                        x_out(G_, s)
                        continue
                    ready(G_, s)

                    def product(k):
                        hi, lo, out = (OH, OL, G[1]) if k < H else (CH, CL, MB[s // 2])
                        if s == 1 and k == 0:
                            pe.wait_ge(ol_dn, 1)
                        if s == 1 and k >= H and k % 4 == 0:
                            pe.wait_ge(cl_dn, k - H + 4)
                        return split_mm(out[:, 0:NQ], s, k, hi[:, k % H, :], lo[:, k % H, :], k % H == 0, k % H == H - 1)

                    products(G_, s, range(KT), KT, product)

            loop(pe, GN["merge"], merge)

            pe.wait_ge(ev[1], 2 * G0["out"] + 1)
            total_sq = MB[0][:, 0:NQ]
            zero(total_sq, True)

            def split_hidden(G_, s, kt=KT, ready_sem=ml_dn, ready_from=0):
                unit(G_, s, NQ, lambda k: MH[:, k, :], lambda k: ML[:, k, :], kt, ready_sem, ready_from)

            def squares(g, s):
                pe.wait_ge(h_sq, g * 4 + (s + 1))
                mm(total_sq, ones[:], sq2[:, s % 2, :], False, False).then_inc(h_st, 1)

            lagged_all(GN["out"], lambda g, s: split_hidden(G0["out"] + g, s), squares)
            zero(total_sq, False).then_inc(h_st, 1)

            for n, (k0, m) in enumerate(PARTS):
                def gu(g):
                    for s in range(4):
                        unit(G0[f"gu{n}"] + g, s, NQ, lambda k: XH[:, k, 0:NQ], lambda k: XL[:, k, 0:NQ], KT, xl_dn)

                loop(pe, GN[f"gu{n}"], gu)

                def dn(g):
                    for s in range(4):
                        split_hidden(G0[f"dn{n}"] + g, s, m, al_dn, k0)

                def y_by_token(g, s):
                    pe.wait_ge(ev[s % 2], 2 * (G0[f"dn{n}"] + g) + (s // 2 + 2))
                    pe.wait_ge(y_cp, g * 4 + (s + 1))
                    for i, (t, w) in enumerate(QTILES):
                        ins = tr(MB[s % 2][0:w, P * i:P * i + P], at2[:, s % 2, t:t + w])
                    ins.then_inc(y_tr, 1)

                if n < len(PARTS) - 1:
                    loop(pe, GN[f"dn{n}"], dn)
                else:
                    pe.wait_ge(rf_sq, 1)
                    lagged_all(GN[f"dn{n}"], lambda g, s: split_hidden(G0[f"dn{n}"] + g, s, m, al_dn, k0), y_by_token)


_INS = ["x_prompt", "x_sample", "cache_k", "cache_v", "cache_ik", "state_conv", "page_table", "meta_tokens", "rel_bias",
        "norm_mix_g", "w_in", "q_norm_g", "k_norm_g", "w_attn_br", "w_dw", "b_dw", "ln_conv_g", "ln_conv_b", "w_conv_br",
        "w_out", "norm_ffn_g", "w_ffn_gate", "w_ffn_up", "w_ffn_down"]
_OUTS = [("y_prompt", (1, SEQ, D)), ("y_sample", (B, Q, D)), ("k_prompt", (1, 1, NP, H, P)), ("v_prompt", (1, 1, NP, H, P)),
         ("ik_prompt", (1, 1, NP, ID)), ("conv_prompt", (1, 1, CTX, CC)), ("k_sample", (1, B, Q, H, P)),
         ("v_sample", (1, B, Q, H, P)), ("ik_sample", (1, B, Q, ID)), ("conv_sample", (1, B, CTX, CC))]


def _constants():
    import math
    import numpy as np

    def bucket(rel):
        n = np.maximum(rel, 0)
        exact = BUCKETS // 2
        nf = np.maximum(n, 1).astype(np.float32)
        large = exact + (np.log(nf / np.float32(exact)) / np.float32(math.log(MAX_DIST / exact)) * np.float32(BUCKETS - exact)).astype(np.int32)
        return np.where(n < exact, n, np.minimum(large, BUCKETS - 1))

    p, q, y = np.arange(P), np.arange(Q), np.arange(RELW)
    j = np.arange(NS) % Q
    rel = np.concatenate([NP - 1 - y, (P + q[:, None] - p[None, :]).ravel(), np.maximum(q[:, None] - j[None, :], 0).ravel(),
                          np.full(P, PAST)])
    assert rel.size == OH_N
    oh = np.zeros((BUCKETS + 1, OH_N), np.float32)
    oh[np.where(rel < 0, BUCKETS, bucket(rel)), np.arange(OH_N)] = 1
    row = np.arange(NS)
    seen = lambda ok: np.where(ok, np.float32(3.4e38), np.float32(OUT_OF_REACH)).astype(np.float32)
    qt, key = np.arange(2)[None, :, None], np.arange(NP)[None, None, :]
    return {
        "c_ident": np.eye(P, dtype=np.float32),
        "c_oh": oh,
        "c_esel": (np.arange(IH)[:, None] == p[None, :] // Q).astype(np.float32),
        "c_qm": (p[:, None] % Q == q[None, :]).astype(np.float32),
        "c_cms": seen(q[None, :] <= row[:, None] % Q),
        "c_cmp": seen(key <= N_META + P * qt + p[:, None, None]),
        "c_blk": np.where((row[:, None] // Q == row[None, :] // Q) & (row[:, None] % Q <= row[None, :] % Q), 0, NEG).astype(np.float32),
        "c_rep": (q[:, None] == row[None, :] % Q).astype(np.float32),
    }


def kernel(**inputs):
    import numpy as np
    import concourse.bacc as bacc
    from concourse.bass_utils import run_bass_kernel_spmd as run

    nc = bacc.Bacc("TRN2", target_bir_lowering=False, num_devices=1)
    arrays, ins, outs = {}, {}, {}
    given = {name: np.ascontiguousarray(inputs[name]) for name in _INS}
    for name, a in {**given, **_constants()}.items():
        arrays[f"in_{name}"] = a
        ins[name] = nc.dram_tensor(f"in_{name}", a.shape, mybir.dt.from_np(a.dtype), kind="ExternalInput").ap()
    for i, (name, shape) in enumerate(_OUTS):
        outs[name] = nc.dram_tensor(f"out_{i}", shape, F32, kind="ExternalOutput").ap()
    layer(nc, ins, outs)
    r = run(nc, [arrays], core_ids=[0])
    return tuple(r.results[0][f"out_{i}"] for i in range(len(_OUTS)))
```
